# Optimizing a Trainium2 kernel written in Bass

```python
import math
import jax, jax.numpy as jnp
from jax import lax
import numpy as np

D_MODEL = 1024
BATCH = 1
SEQ = 256
DEPTH = 2

HEAD_DIM = 64
N_MIX_HEADS = 12
SWA_KV_HEADS = 3
SWA_WINDOW = 128
DIL_GROUPS = ((128, 1), (512, 4), (2048, 16))
DIL_HEADS = 4
MAX_DIL = 16
N_MEM = 256
MEM_HEADS = 4
BLOCK = 128
N_BUCKETS = 32
MAX_DISTANCE = 2048
D_FF = 3584
N_EXPERTS = 8
TOP_K = 2
EPS = 1e-5
NEG = -1e30

SWA_IN = N_MIX_HEADS * HEAD_DIM + 2 * SWA_KV_HEADS * HEAD_DIM + MEM_HEADS * HEAD_DIM
DIL_IN = len(DIL_GROUPS) * 3 * DIL_HEADS * HEAD_DIM + MEM_HEADS * HEAD_DIM
SWA_CAT = N_MIX_HEADS * HEAD_DIM + MEM_HEADS * HEAD_DIM
DIL_CAT = DIL_HEADS * HEAD_DIM + MEM_HEADS * HEAD_DIM

kernel_name = "hybrid_swa_sink_dilated_moe_trunk"

def rmsnorm(x, g):
    xf = x.astype(jnp.float32)
    y = xf * lax.rsqrt(jnp.mean(xf * xf, axis=-1, keepdims=True) + EPS)
    return (y * g.astype(jnp.float32)).astype(x.dtype)

def t5_bucket(dist):
    max_exact = N_BUCKETS // 2
    d = jnp.maximum(dist, 0)
    ratio = jnp.maximum(d, 1).astype(jnp.float32) / max_exact
    large = max_exact + (jnp.log(ratio) / math.log(MAX_DISTANCE / max_exact)
                         * (N_BUCKETS - max_exact)).astype(jnp.int32)
    return jnp.where(d < max_exact, d, jnp.minimum(large, N_BUCKETS - 1))

def rel_bias(table, dist_tok, heads):
    b = table[t5_bucket(dist_tok)][..., heads]
    return jnp.moveaxis(b, -1, 0).astype(jnp.float32)

def band_offsets():
    qi = jnp.arange(BLOCK)[:, None]
    kj = jnp.arange(2 * BLOCK)[None, :]
    return qi + BLOCK - kj

def banded_attention(q, k, v, bias, max_dist, sink):
    nb = q.shape[2]
    shift = lambda a: jnp.pad(a, ((0, 0), (0, 0), (1, 0)) + ((0, 0),) * (a.ndim - 3))[:, :, :-1]
    kk = jnp.concatenate([shift(k), k], axis=3)
    vv = jnp.concatenate([shift(v), v], axis=3)
    dist = band_offsets()
    kj = jnp.arange(2 * BLOCK)
    has_prev = (jnp.arange(nb) > 0)[:, None, None] | (kj >= BLOCK)[None, None, :]
    valid = (dist >= 0) & (dist <= max_dist) & has_prev
    s = jnp.einsum('brnqhgd,brnkhd->brnhgqk', q * (HEAD_DIM ** -0.5), kk).astype(jnp.float32) + bias
    s = jnp.where(valid[:, None, None], s, NEG)
    m = jnp.max(s, axis=-1)
    if sink is not None:
        m = jnp.maximum(m, sink[:, :, None])
    p = jnp.exp(s - m[..., None])
    denom = jnp.sum(p, axis=-1)
    if sink is not None:
        denom = denom + jnp.exp(sink[:, :, None] - m)
    p = p / denom[..., None]
    o = jnp.einsum('brnhgqk,brnkhd->brnqhgd', p.astype(vv.dtype), vv)
    return o, m + jnp.log(denom)

def to_dilated(a, d):
    B, sp = a.shape[:2]
    a = a.reshape(B, sp // d, d, *a.shape[2:])
    a = jnp.swapaxes(a, 1, 2)
    return a.reshape(B, d, sp // (d * BLOCK), BLOCK, *a.shape[3:])

def from_dilated(a):
    B, d, nb, L = a.shape[:4]
    a = a.reshape(B, d, nb * L, *a.shape[4:])
    a = jnp.swapaxes(a, 1, 2)
    return a.reshape(B, nb * L * d, *a.shape[3:])

def memory_attention(qm, mem_n, w_mem_kv):
    B, S, _ = qm.shape
    kv = jnp.einsum('bmd,de->bme', mem_n, w_mem_kv).reshape(B, mem_n.shape[1], 2, MEM_HEADS, HEAD_DIM)
    q = qm.reshape(B, S, MEM_HEADS, HEAD_DIM) * (HEAD_DIM ** -0.5)
    s = jnp.einsum('bshd,bmhd->bhsm', q, kv[:, :, 0]).astype(jnp.float32)
    p = jax.nn.softmax(s, axis=-1).astype(qm.dtype)
    return jnp.einsum('bhsm,bmhd->bshd', p, kv[:, :, 1]).reshape(B, S, MEM_HEADS * HEAD_DIM)

def swa_sink_mixer(h, mem_n, table, w_in, sinks, w_mem_kv, w_out):
    B, S, _ = h.shape
    nb = S // BLOCK
    g = N_MIX_HEADS // SWA_KV_HEADS
    dq, dkv = N_MIX_HEADS * HEAD_DIM, SWA_KV_HEADS * HEAD_DIM
    p = jnp.einsum('bsd,de->bse', h, w_in)
    q, k, v, qm = jnp.split(p, [dq, dq + dkv, dq + 2 * dkv], axis=-1)
    q = q.reshape(B, 1, nb, BLOCK, SWA_KV_HEADS, g, HEAD_DIM)
    k = k.reshape(B, 1, nb, BLOCK, SWA_KV_HEADS, HEAD_DIM)
    v = v.reshape(B, 1, nb, BLOCK, SWA_KV_HEADS, HEAD_DIM)
    bias = rel_bias(table, band_offsets(), slice(0, N_MIX_HEADS)).reshape(SWA_KV_HEADS, g, BLOCK, 2 * BLOCK)
    o, _ = banded_attention(q, k, v, bias, SWA_WINDOW - 1,
                            sinks.astype(jnp.float32).reshape(SWA_KV_HEADS, g))
    o = o.reshape(B, S, dq)
    om = memory_attention(qm, mem_n, w_mem_kv)
    return jnp.einsum('bse,ed->bsd', jnp.concatenate([o, om], axis=-1), w_out)

def dilated_mixer(h, mem_n, table, w_in, w_mem_kv, w_out):
    B, S, _ = h.shape
    n_grp = len(DIL_GROUPS)
    dg = 3 * DIL_HEADS * HEAD_DIM
    p = jnp.einsum('bsd,de->bse', h, w_in)
    pg, qm = p[..., :n_grp * dg], p[..., n_grp * dg:]
    unit = MAX_DIL * BLOCK
    sp = -(-S // unit) * unit
    pg = jnp.pad(pg, ((0, 0), (0, sp - S), (0, 0))).reshape(B, sp, n_grp, 3, DIL_HEADS, HEAD_DIM)
    outs, lses = [], []
    for gi, (window, dil) in enumerate(DIL_GROUPS):
        q, k, v = (to_dilated(pg[:, :, gi, c], dil) for c in range(3))
        bias = rel_bias(table, band_offsets() * dil, slice(gi * DIL_HEADS, (gi + 1) * DIL_HEADS))[:, None]
        o, lse = banded_attention(q[:, :, :, :, :, None], k, v, bias, window // dil, None)
        outs.append(from_dilated(o[..., 0, :]))
        lses.append(from_dilated(jnp.moveaxis(lse[..., 0, :], -1, 3)))
    w = jax.nn.softmax(jnp.stack(lses), axis=0)
    o = jnp.sum(w[..., None] * jnp.stack(outs).astype(jnp.float32), axis=0)[:, :S]
    o = o.astype(h.dtype).reshape(B, S, DIL_HEADS * HEAD_DIM)
    om = memory_attention(qm, mem_n, w_mem_kv)
    return jnp.einsum('bse,ed->bsd', jnp.concatenate([o, om], axis=-1), w_out)

def swiglu(h, w_gate, w_up, w_down):
    a = jnp.einsum('bsd,df->bsf', h, w_gate)
    b = jnp.einsum('bsd,df->bsf', h, w_up)
    return jnp.einsum('bsf,fd->bsd', jax.nn.silu(a) * b, w_down)

def moe_swiglu(h, router, w_gate, w_up, w_down):
    logits = jnp.einsum('bsd,de->bse', h, router).astype(jnp.float32)
    vals, idx = lax.top_k(logits, TOP_K)
    gates = jax.nn.softmax(vals, axis=-1)
    combine = jnp.sum(jax.nn.one_hot(idx, N_EXPERTS, dtype=jnp.float32) * gates[..., None], axis=-2)
    y = jnp.zeros_like(h)
    for e in range(N_EXPERTS):
        y = y + combine[..., e:e + 1].astype(h.dtype) * swiglu(h, w_gate[e], w_up[e], w_down[e])
    return y

def setup_inputs(seed: int = 0) -> dict:
    key = jax.random.key(seed)
    ks = iter(jax.random.split(key, 32))
    f32 = jnp.float32
    n_even, n_odd = (DEPTH + 1) // 2, DEPTH // 2

    def nrm(shape, scale):
        return jax.random.normal(next(ks), shape, f32) * scale

    def gain(shape):
        return 1.0 + nrm(shape, 0.02)

    d = D_MODEL
    return {
        "x": nrm((BATCH, SEQ, d), 1.0),
        "mem": nrm((BATCH, N_MEM, d), 1.0),
        "rel_bias_table": nrm((N_BUCKETS, N_MIX_HEADS), 0.2),
        "mem_norm": gain((d,)),
        "norm_mix": gain((DEPTH, d)),
        "norm_ffn": gain((DEPTH, d)),
        "final_norm": gain((d,)),
        "swa_w_in": nrm((n_even, d, SWA_IN), d ** -0.5),
        "swa_sinks": nrm((n_even, N_MIX_HEADS), 0.5),
        "swa_w_mem_kv": nrm((n_even, d, 2 * MEM_HEADS * HEAD_DIM), d ** -0.5),
        "swa_w_out": nrm((n_even, SWA_CAT, d), SWA_CAT ** -0.5),
        "dil_w_in": nrm((n_odd, d, DIL_IN), d ** -0.5),
        "dil_w_mem_kv": nrm((n_odd, d, 2 * MEM_HEADS * HEAD_DIM), d ** -0.5),
        "dil_w_out": nrm((n_odd, DIL_CAT, d), DIL_CAT ** -0.5),
        "ffn_gate": nrm((n_even, d, D_FF), d ** -0.5),
        "ffn_up": nrm((n_even, d, D_FF), d ** -0.5),
        "ffn_down": nrm((n_even, D_FF, d), D_FF ** -0.5),
        "router": nrm((n_odd, d, N_EXPERTS), d ** -0.5),
        "moe_gate": nrm((n_odd, N_EXPERTS, d, D_FF), d ** -0.5),
        "moe_up": nrm((n_odd, N_EXPERTS, d, D_FF), d ** -0.5),
        "moe_down": nrm((n_odd, N_EXPERTS, D_FF, d), D_FF ** -0.5),
    }

def reference(x, mem, rel_bias_table, mem_norm, norm_mix, norm_ffn, final_norm,
              swa_w_in, swa_sinks, swa_w_mem_kv, swa_w_out,
              dil_w_in, dil_w_mem_kv, dil_w_out,
              ffn_gate, ffn_up, ffn_down,
              router, moe_gate, moe_up, moe_down):
    h = x
    mem_n = rmsnorm(mem, mem_norm)
    for i in range(DEPTH):
        j = i // 2
        hn = rmsnorm(h, norm_mix[i])
        if i % 2 == 0:
            h = h + swa_sink_mixer(hn, mem_n, rel_bias_table, swa_w_in[j], swa_sinks[j],
                                   swa_w_mem_kv[j], swa_w_out[j])
            h = h + swiglu(rmsnorm(h, norm_ffn[i]), ffn_gate[j], ffn_up[j], ffn_down[j])
        else:
            h = h + dilated_mixer(hn, mem_n, rel_bias_table, dil_w_in[j], dil_w_mem_kv[j], dil_w_out[j])
            h = h + moe_swiglu(rmsnorm(h, norm_ffn[i]), router[j], moe_gate[j], moe_up[j], moe_down[j])
    return rmsnorm(h, final_norm)


_drawn_inputs = setup_inputs


def setup_inputs(seed=0):
    import zlib

    import numpy as np

    out = dict(_drawn_inputs(seed))
    spreads = {}
    factors = {'mem_norm': 6.672,
     'norm_mix': 5.164,
     'final_norm': 7.513,
     'swa_sinks': 6.37,
     'norm_ffn': 3.579}
    for name, (base, spread) in spreads.items():
        noise = np.random.default_rng([zlib.crc32(name.encode()), seed]).standard_normal(out[name].shape)
        drawn = base * np.exp(spread * noise) if base else spread * noise
        out[name] = __import__('jax').numpy.asarray(drawn.astype(out[name].dtype))
    for name, factor in factors.items():
        out[name] = (out[name] * factor).astype(out[name].dtype)
    return out
```

```python
from contextlib import ExitStack

import numpy as np

import concourse.bass as bass
from concourse import mybir

F32 = mybir.dt.float32
F32R = mybir.dt.float32r
I32 = mybir.dt.int32
ACT = mybir.ActivationFunctionType
ALU = mybir.AluOpType
AX = mybir.AxisListType

P = 128
D = 1024
SEQ = 256
TILES = SEQ // P
KT = D // P
DFF = 3584
FCH = 512
STEPS = DFF // FCH
FT = FCH // P
NE = 8
HD = 64
NH = 12
MH = 4
ITEMS = NH + MH
NEG = -1e30
EPS = 1e-5
RAW = 6
CUT = 3
UNIT = 2048
SWA_IN = 1408
DIL_IN = 2560
MAX_OVER = (2 * SEQ) // (P + 1)
JOBS = NE + MAX_OVER
COLS = JOBS + 1
RLEN = 3 * P

CHUNKS = (
    [("mk0", 512, 8, 0), ("mk1", 512, 8, 0)]
    + [("si", min(512, SWA_IN - o), 8, o) for o in range(0, SWA_IN, 512)]
    + [("so", 512, 8, o) for o in range(0, D, 512)]
    + [("di", 512, 8, o) for o in range(0, DIL_IN, 512)]
    + [("do", 512, 4, o) for o in range(0, D, 512)]
)
FFN_UNITS = STEPS * 6


def plan_units():
    first, n, ffn = [], 0, None
    for name, _, rows, _ in CHUNKS:
        if name == "di" and ffn is None:
            ffn, n = n, n + FFN_UNITS
        first.append(n)
        n += rows // 4
    return first, ffn, n


FIRST, FFN0, MOE0 = plan_units()
C_SI, C_SO, C_DI, C_DO = 2, 5, 7, 12
ACT_EV = [sum(CHUNKS[i][0] not in ("so", "do") for i in range(c + 1)) for c in range(len(CHUNKS))]
DVE_EV = [sum(2 if CHUNKS[i][0] in ("so", "do") else 1 for i in range(c + 1)) for c in range(len(CHUNKS))]
TR_BANKS = [4, 4, 4, 4, 4, 2, 4]
TR0 = [sum(TR_BANKS[:i]) for i in range(len(TR_BANKS) + 1)]
T_MEM, T_MIX0, T_CAT0, T_FFN0, T_MIX1, T_CAT1, T_ROUTE = range(7)
XT_FREE = [0, FIRST[C_SI], FIRST[C_SO], FFN0, FIRST[C_DI], FIRST[C_DO]]
EV_MOE = TILES * STEPS


def t5_bucket(dist):
    d = np.maximum(dist, 0)
    ratio = np.maximum(d, 1).astype(np.float32) / np.float32(16)
    large = 16 + (np.log(ratio).astype(np.float32) / np.float32(np.log(2048 / 16)) * 16).astype(np.int32)
    return np.where(d < 16, d, np.minimum(large, 31))


def shape_constants():
    c = np.zeros((P, 5 * P + 80), np.float32)
    i = np.arange(P)
    c[:, 0:P] = np.eye(P)
    c[:, P:2 * P] = np.eye(P)[::-1]
    c[:, 2 * P:3 * P] = i[:, None] < i[None, :]
    c[:, 3 * P:4 * P] = 1.0
    c[:, 4 * P:5 * P] = i[None, :]
    e = np.arange(NE)
    c[:, 5 * P:5 * P + 64] = (e[None, :] < e[:, None]).reshape(-1)
    c[:, 5 * P + 64] = EPS
    c[:, 5 * P + 65:5 * P + 73] = e
    dist = 2 * P - 1 - np.arange(RLEN)
    one = np.zeros((33, 4, RLEN), np.float32)
    b = t5_bucket(dist)
    for g, (most, dil) in enumerate([(127, 1), (128, 1), (512, 4), (2048, 16)]):
        one[b, g, np.arange(RLEN)] = 1.0
        ok = (dist >= 0) & (dist <= most) & (dist % dil == 0)
        one[32, g] = np.where(ok, 0.0, NEG)
    return c, one


def wait(eng, sem, value):
    if not isinstance(value, int) or value > 0:
        eng.wait_ge(sem, value)


def free(ap, *dims):
    return bass.AP(ap.tensor, ap.offset, [list(ap.ap[0])] + [list(d) for d in dims])


def trunk(nc, x, mem, rel_bias_table, mem_norm, norm_mix, norm_ffn, final_norm, swa_w_in, swa_sinks,
          swa_w_mem_kv, swa_w_out, dil_w_in, dil_w_mem_kv, dil_w_out, ffn_gate, ffn_up, ffn_down, router,
          moe_gate, moe_up, moe_down, index_mats, bias_onehot, out):
    chunk_w = {
        "mk0": swa_w_mem_kv, "mk1": dil_w_mem_kv, "si": swa_w_in, "so": swa_w_out, "di": dil_w_in, "do": dil_w_out,
    }
    chunk_w = {k: v.rearrange("z (k p) f -> p (z k) f", p=P) for k, v in chunk_w.items()}
    ffn_in = [w.rearrange("z (k p) f -> p (z k) f", p=P) for w in (ffn_up, ffn_gate)]
    ffn_out = ffn_down.rearrange("z (k p) f -> p (z k) f", p=P)
    moe_in = [w.rearrange("z e (k p) f -> p (z e) k f", p=P) for w in (moe_up, moe_gate)]
    moe_out = moe_down.rearrange("z e (k p) f -> p (z e) k f", p=P)
    gains = [mem_norm, norm_mix[0, :], norm_ffn[0, :], norm_mix[1, :], norm_ffn[1, :], final_norm]

    bias_rows = [nc.dram_tensor(f"bias_rows_{i}", (NH, RLEN), F32, kind="Internal").ap() for i in range(2)]

    ctx = ExitStack()
    with ctx:
        def sb(name, shape, dt=F32, scope=ctx):
            return scope.enter_context(nc.sbuf_tensor(name, shape, dt))

        def sem(name):
            return ctx.enter_context(nc.semaphore(name))

        raw = sb("raw", [P, RAW, UNIT])
        whi = sb("whi", [P, CUT, UNIT], F32R)
        wlo = sb("wlo", [P, CUT, UNIT], F32R)
        h = sb("h", [P, TILES, D])
        hn = sb("hn", [P, TILES, D])
        xhi = sb("xhi", [P, KT, SEQ], F32R)
        xlo = sb("xlo", [P, KT, SEQ], F32R)
        gain = sb("gain", [P, 2, D])
        memkv = sb("memkv", [P, 2, TILES, 512])
        mats = sb("mats", [P, 5 * P + 80])
        stats = sb("stats", [P, 64])
        squares = sb("squares", [P, D])
        ident, anti, before, ones, iota = (mats[:, i * P:(i + 1) * P] for i in range(5))
        tri, eps, expert_no = mats[:, 640:704], mats[:, 704:705], mats[:, 705:713]
        ssq, std, rstd = stats[:, 0:12], stats[:, 16:28], stats[:, 32:44]

        with ExitStack() as mix:
            proj = sb("proj", [P, TILES, DIL_IN], scope=mix)
            bias = sb("bias", [P, NH, SEQ], scope=mix)
            qk = sb("qk", [HD, 2, 512], scope=mix)
            probs = sb("probs", [P, 2, 512], scope=mix)
            probsT = sb("probsT", [P, 2, 512], scope=mix)
            oraw = sb("oraw", [P, TILES, ITEMS, HD], scope=mix)
            sm = sb("sm", [P, 512], scope=mix)
        with ExitStack() as glu:
            thi = sb("thi", [P, FT, SEQ], F32R, scope=glu)
            tlo = sb("tlo", [P, FT, SEQ], F32R, scope=glu)
            silu = sb("silu", [P, TILES, FCH], scope=glu)
            act_h = sb("act_h", [P, TILES, FCH], scope=glu)
            nhi = sb("nhi", [P, TILES, D], F32R, scope=glu)
            nlo = sb("nlo", [P, TILES, D], F32R, scope=glu)
            yhi = sb("yhi", [P, D], F32R, scope=glu)
            ylo = sb("ylo", [P, D], F32R, scope=glu)
            zero = sb("zero", [P, 512], F32R, scope=glu)
            pick = sb("pick", [P, TILES, P], F32R, scope=glu)
            put_next = sb("put_next", [P, SEQ], scope=glu)
            put = sb("put", [P, SEQ], F32R, scope=glu)
            gate_next = sb("gate_next", [P, 1], scope=glu)
            gate = sb("gate", [P, 1], scope=glu)
            rt = sb("rt", [P, 1024], scope=glu)
            rw = sb("rw", [P, KT, NE], scope=glu)
            pos = sb("pos", [P, TILES, COLS], scope=glu)
            comb = sb("comb", [P, TILES, COLS], scope=glu)
            jobs_i = sb("jobs_i", [1, 8], I32, scope=glu)
        with ExitStack() as early:
            onehot = sb("onehot", [33, 4, RLEN], scope=early)
            table = sb("table", [33, NH], scope=early)
            rows = sb("rows", [NH, 4, RLEN], scope=early)
        xtf = memkv[:, :, :, :].rearrange("p l t c -> p (l t c)").rearrange("p (k t) -> p k t", k=KT)
        ps = ctx.enter_context(nc.psum_tensor("ps", [P, 8, 512], F32))

        mem_in, x_in, const_in, out_done = sem("mem_in"), sem("x_in"), sem("const_in"), sem("out_done")
        onehot_in, table_in, sink_in, rw_in = sem("onehot_in"), sem("table_in"), sem("sink_in"), sem("rw_in")
        gain_in = [sem("gain_in0"), sem("gain_in1")]
        raw_full = [sem(f"raw_full{i}") for i in range(RAW)]
        hi_ready, lo_ready, units_done = sem("hi_ready"), sem("lo_ready"), sem("units_done")
        table_one, rows_mm, rows_sb, rows_out, bias_in = (
            sem("table_one"), sem("rows_mm"), sem("rows_sb"), sem("rows_out"), sem("bias_in"))
        sq_done, std_done, rstd_done, hn_done = sem("sq_done"), sem("std_done"), sem("rstd_done"), sem("hn_done")
        tr_done, xhi_ready, xlo_ready = sem("tr_done"), sem("xhi_ready"), sem("xlo_ready")
        chunk_done, ev_act, ev_dve = sem("chunk_done"), sem("ev_act"), sem("ev_dve")
        qkT_done, qk_ready, s_done, nmr_done, nm_ready = (
            sem("qkT_done"), sem("qk_ready"), sem("s_done"), sem("nmr_done"), sem("nm_ready"))
        p_ready, pT_done, pT_ready, o_done, o_out = (
            sem("p_ready"), sem("pT_done"), sem("pT_ready"), sem("o_done"), sem("o_out"))
        fexp_in, fexp_out, cat_done = sem("fexp_in"), sem("fexp_out"), sem("cat_done")
        dve_chain = sem("dve_chain")
        g_done, silu_ready, act_ready, t_done, thi_ready, tlo_ready = (
            sem("g_done"), sem("silu_ready"), sem("act_ready"), sem("t_done"), sem("thi_ready"), sem("tlo_ready"))
        zero_set, y_clear, ffn_added = sem("zero_set"), sem("y_clear"), sem("ffn_added")
        xtf_ready, logit_done, top_in, top_exp, rank_in, rank_done, table_ready = (
            sem("xtf_ready"), sem("logit_done"), sem("top_in"), sem("top_exp"), sem("rank_in"), sem("rank_done"),
            sem("table_ready"))
        nhi_ready, nlo_ready = sem("nhi_ready"), sem("nlo_ready")
        pick_ready, gx_done, put_done, gxhi, gxlo, put_out, put_now = (
            sem("pick_ready"), sem("gx_done"), sem("put_done"), sem("gxhi"), sem("gxlo"), sem("put_out"),
            sem("put_now"))
        yhi_ready, ylo_ready, sc_done, h_added = sem("yhi_ready"), sem("ylo_ready"), sem("sc_done"), sem("h_added")
        block = ctx.enter_context(nc.Block())

        items = [[], []]
        for i in range(NH):
            items[0].append((i * HD, 768 + i // 4 * HD, 960 + i // 4 * HD))
            base = i // 4 * 768 + i % 4 * HD
            items[1].append((base, base + 256, base + 512))
        for m in range(MH):
            items[0].append((1152 + m * HD, m * HD, 256 + m * HD))
            items[1].append((2304 + m * HD, m * HD, 256 + m * HD))

        def kv(layer, i, t, col):
            src = proj[:, t, col:col + HD] if i < NH else memkv[:, layer, t, col:col + HD]
            return src

        B_U, B_G, B_Y = (0, 1), (2, 3), ((4, 5), (6, 7))
        B_X, B_PUT, B_SC = (6, 7), 3, (1, 3, 6, 7)

        def uses(c, rounds):
            return c // RAW + 1 + rounds

        def span(c):
            for k, (_, width, rows_, _) in enumerate(CHUNKS):
                if FIRST[k] <= c < FIRST[k] + rows_ // 4:
                    return 4 * width
            return UNIT

        @block.sync
        def _(sp):
            sp.dma_start(hn[:, :, :], mem[0].rearrange("(t p) d -> p t d", p=P)).then_inc(mem_in, 16)
            sp.dma_start(h[:, :, :], x[0].rearrange("(t p) d -> p t d", p=P)).then_inc(x_in, 16)

            def load(c, rounds, src):
                wait(sp, lo_ready, c + RAW * rounds - RAW + 1)
                dst = raw[:, c % RAW, 0:span(c)].rearrange("p (k f) -> p k f", k=src.shape[-2])
                sp.dma_start(dst, src).then_inc(raw_full[c % RAW], 16)

            def load_chunks(lo, hi):
                for k in range(lo, hi):
                    name, width, rows_, off = CHUNKS[k]
                    for i in range(rows_ // 4):
                        load(FIRST[k] + i, 0, chunk_w[name][:, 4 * i:4 * i + 4, off:off + width])

            load_chunks(0, C_DI)
            for i in range(4):
                load(FFN0 + i, 0, ffn_in[i // 2][:, i % 2 * 4:i % 2 * 4 + 4, 0:FCH])
            with sp.Fori(1, STEPS) as s:
                for i in range(4):
                    load(FFN0 - 2 + i, s, ffn_in[i // 2][:, i % 2 * 4:i % 2 * 4 + 4, bass.ds(s * FCH, FCH)])
                for i in range(2):
                    load(FFN0 + 2 + i, s, ffn_out[:, bass.ds(s * FT - FT + 2 * i, 2), :])
            for i in range(2):
                load(FFN0 + FFN_UNITS - 2 + i, 0, ffn_out[:, (STEPS - 1) * FT + 2 * i:(STEPS - 1) * FT + 2 * i + 2, :])
            load_chunks(C_DI, len(CHUNKS))

            def load_expert(job, e):
                for i in range(4):
                    load(MOE0 + i, STEPS * job, moe_in[i // 2][:, bass.ds(e, 1), i % 2 * 4:i % 2 * 4 + 4, 0:FCH])
                with sp.Fori(1, STEPS) as s:
                    for i in range(4):
                        load(MOE0 - 2 + i, job * STEPS + s,
                             moe_in[i // 2][:, bass.ds(e, 1), i % 2 * 4:i % 2 * 4 + 4, bass.ds(s * FCH, FCH)])
                    for i in range(2):
                        load(MOE0 + 2 + i, job * STEPS + s,
                             moe_out[:, bass.ds(e, 1), bass.ds(s * FT - FT + 2 * i, 2), :])
                for i in range(2):
                    f = (STEPS - 1) * FT + 2 * i
                    load(MOE0 + FFN_UNITS - 2 + i, STEPS * job, moe_out[:, bass.ds(e, 1), f:f + 2, :])

            with sp.Fori(0, NE) as job:
                load_expert(job, job)
            sp.wait_ge(table_ready, 1)
            n_over = sp.value_load(jobs_i[0:1, 1:2], min_val=0, max_val=MAX_OVER)
            with sp.If(n_over > 0):
                with sp.Fori(0, n_over) as o:
                    e = sp.value_load(jobs_i[0:1, bass.ds(o + 2, 1)], min_val=0, max_val=NE - 1)
                    load_expert(o + NE, e)
            for t in range(TILES):
                sp.wait_ge(hn_done, 2 * 5 + t + 1)
                sp.dma_start(out[0, t * P:(t + 1) * P, :], hn[:, t, :]).then_inc(out_done, 16)
            sp.wait_ge(out_done, 16 * TILES)

        @block.gpsimd
        def _(pool):
            def load_gain(k):
                if k >= 2:
                    pool.wait_ge(hn_done, 2 * (k - 2) + 2)
                pool.dma_start(gain[:, k % 2, :], bass.AP(gains[k].tensor, gains[k].offset, [[0, P], [1, D]]))\
                    .then_inc(gain_in[k % 2], 16)

            load_gain(0)
            load_gain(1)
            pool.dma_start(sm[:, 496:508], bass.AP(swa_sinks.tensor, swa_sinks.offset, [[0, P], [1, NH]]))\
                .then_inc(sink_in, 16)
            pool.wait_ge(rows_sb, 4)
            pool.dma_start(bias_rows[0], rows[0:NH, 0, :]).then_inc(rows_out, 16)
            for g in range(3):
                pool.dma_start(bias_rows[1][4 * g:4 * g + 4, :], rows[0:4, 1 + g, :]).then_inc(rows_out, 16)
            pool.wait_ge(rows_out, 64)

            def load_bias(layer):
                b = bias_rows[layer]
                for n in range(3):
                    src = bass.AP(b.tensor, b.offset + 4 * n * RLEN, [[1, P], [RLEN, 4], [1, SEQ]])
                    pool.dma_start(bias[:, 4 * n:4 * n + 4, :], src).then_inc(bias_in, 16)

            load_bias(0)
            load_gain(2)
            load_gain(3)
            pool.wait_ge(s_done, ITEMS)
            load_bias(1)
            load_gain(4)
            pool.wait_ge(cat_done, 4)
            pool.dma_start(rw[:, :, :], router[0].rearrange("(k p) e -> p k e", p=P)).then_inc(rw_in, 16)
            load_gain(5)

        @block.scalar
        def _(act):
            act.dma_start(mats[:, :], index_mats).then_inc(const_in, 16)
            act.dma_start(onehot[:, :, :], bias_onehot).then_inc(onehot_in, 16)
            act.dma_start(table[0:32, :], rel_bias_table).then_inc(table_in, 16)

            nxt = [0]

            def cut(c, rounds):
                act.wait_ge(raw_full[c % RAW], 16 * uses(c, rounds))
                wait(act, units_done, c + RAW * rounds - CUT + 1)
                act.activation(whi[:, c % CUT, 0:span(c)], raw[:, c % RAW, 0:span(c)], ACT.Copy).then_inc(hi_ready, 1)

            def cut_upto(n):
                while nxt[0] < n:
                    cut(nxt[0], 0)
                    nxt[0] += 1

            def norm_sums(k, src):
                for t in range(TILES):
                    wait(act, sq_done, 2 * k + t)
                    act.activation(squares[:, :], src[:, t, :], ACT.Square,
                                   accum_out=ssq[:, 2 * k + t:2 * k + t + 1]).then_inc(sq_done, 1)
                act.wait_ge(sq_done, 2 * k + 2)
                act.activation(std[:, 2 * k:2 * k + 2], ssq[:, 2 * k:2 * k + 2], ACT.Sqrt, bias=eps, scale=1.0 / D)\
                    .then_inc(std_done, 1)

            def xT_hi(op):
                wait(act, units_done, XT_FREE[op])
                for b in range(TR_BANKS[op]):
                    act.wait_ge(tr_done, TR0[op] + b + 1)
                    act.activation(xhi[:, 2 * b:2 * b + 2, :], ps[:, b, :].rearrange("p (k t) -> p k t", k=2), ACT.Copy)\
                        .then_inc(xhi_ready, 1)

            def chunk_out(c, dst):
                cut_upto(FIRST[c] + CHUNKS[c][2] // 4 + 2)
                act.wait_ge(chunk_done, c + 1)
                act.activation(dst, ps[:, 4 + 2 * (c % 2), 0:CHUNKS[c][1]], ACT.Copy).then_inc(ev_act, 1)

            def attention(layer):
                base = ITEMS * layer
                for n in range(ITEMS + 1):
                    if n < ITEMS:
                        act.wait_ge(qkT_done, base + n + 1)
                        wait(act, s_done, base + n - 1)
                        act.activation(qk[:, n % 2, :], ps[0:HD, 0, :], ACT.Copy).then_inc(qk_ready, 1)
                    if n >= 1:
                        i = n - 1
                        bank = 3 + (base + i) % 3
                        act.wait_ge(nm_ready, base + i + 1)
                        wait(act, pT_done, base + i - 1)
                        w0 = P if i < NH else SEQ
                        for qb, (a, b) in enumerate([(0, w0), (w0, w0 + SEQ)]):
                            act.activation(probs[:, i % 2, a:b], ps[:, bank, a:b], ACT.Exp,
                                           bias=sm[:, 32 + 16 * qb + i:33 + 16 * qb + i], scale=0.125,
                                           accum_out=sm[:, 64 + 16 * qb + i:65 + 16 * qb + i]).then_inc(p_ready, 1)
                act.wait_ge(fexp_in, layer + 1)
                n = 2 * TILES * NH if layer == 0 else TILES * NH
                act.activation(sm[:, 128:128 + n], sm[:, 128:128 + n], ACT.Exp).then_inc(fexp_out, 1)

            def glu_silu(t, ev, signal, value):
                act.wait_ge(signal, value)
                act.activation(silu[:, t, :], ps[:, B_G[t], :], ACT.Silu).then_inc(silu_ready, 1)

            def glu_thi(t, ev, unit):
                act.wait_ge(t_done, ev + 1)
                wait(act, units_done, unit)
                act.activation(thi[:, :, t * P:(t + 1) * P], ps[:, B_G[t], :].rearrange("p (k t) -> p k t", k=FT),
                               ACT.Copy).then_inc(thi_ready, 1)

            act.wait_ge(mem_in, 16)
            act.wait_ge(const_in, 16)
            norm_sums(0, hn)
            act.wait_ge(x_in, 16)
            norm_sums(1, h)
            act.wait_ge(rows_mm, 1)
            for g in range(4):
                n = NH if g == 0 else 4
                act.activation(rows[0:n, g, :], ps[0:n, g, 0:RLEN], ACT.Copy, scale=8.0).then_inc(rows_sb, 1)
            cut_upto(2)
            xT_hi(T_MEM)
            chunk_out(0, memkv[:, 0, 0, :])
            chunk_out(1, memkv[:, 1, 0, :])
            xT_hi(T_MIX0)
            act.wait_ge(rows_out, 64)
            for c in range(C_SI, C_SO):
                chunk_out(c, proj[:, 0, CHUNKS[c][3]:CHUNKS[c][3] + CHUNKS[c][1]])
            attention(0)
            xT_hi(T_CAT0)
            cut_upto(FIRST[C_SO] + 6)
            act.wait_ge(ev_dve, DVE_EV[C_SO + 1])
            norm_sums(2, h)
            xT_hi(T_FFN0)
            for i in range(4):
                cut(FFN0 + 2 + i, 0)
            glu_silu(0, 0, g_done, 1)
            glu_silu(1, 1, units_done, FFN0 + 4)
            for t in range(TILES):
                glu_thi(t, t, FFN0 + 4)
            with act.Fori(1, STEPS) as s:
                for i in range(4):
                    cut(FFN0 + i, s)
                glu_silu(0, s * TILES, g_done, s + 1)
                glu_silu(1, s * TILES + 1, units_done, s * 6 + FFN0 + 2)
                for i in range(2):
                    cut(FFN0 + 4 + i, s)
                for t in range(TILES):
                    glu_thi(t, s * TILES + t, FFN0 + 4 + 6 * s)
            nxt[0] = FFN0 + FFN_UNITS
            cut_upto(FIRST[C_DI] + 2)
            act.wait_ge(ffn_added, 4)
            norm_sums(3, h)
            xT_hi(T_MIX1)
            for c in range(C_DI, C_DO):
                chunk_out(c, proj[:, 0, CHUNKS[c][3]:CHUNKS[c][3] + CHUNKS[c][1]])
            attention(1)
            xT_hi(T_CAT1)
            cut_upto(MOE0)
            act.wait_ge(ev_dve, DVE_EV[-1])
            norm_sums(4, h)
            for b in range(4):
                act.wait_ge(tr_done, TR0[T_ROUTE] + b + 1)
                act.activation(xtf[:, 2 * b:2 * b + 2, :], ps[:, b, :].rearrange("p (k t) -> p k t", k=2), ACT.Copy)\
                    .then_inc(xtf_ready, 1)
            for t in range(TILES):
                act.activation(nhi[:, t, :], hn[:, t, :], ACT.Copy).then_inc(nhi_ready, 1)
            act.wait_ge(top_in, 1)
            act.activation(rt[:, 160:176], rt[:, 160:176], ACT.Exp).then_inc(top_exp, 1)

            def gather_out(q):
                act.wait_ge(put_done, q + 1)
                act.activation(put_next[:, :], ps[:, B_PUT, 0:SEQ], ACT.Copy).then_inc(put_out, 1)
                act.activation(gate_next[:, :], ps[:, B_PUT, SEQ:SEQ + 1], ACT.Copy).then_inc(put_out, 1)
                for b in range(2):
                    act.wait_ge(gx_done, 2 * q + b + 1)
                    act.activation(xhi[:, 4 * b:4 * b + 4, 0:P], ps[:, B_X[b], :].rearrange("p (k t) -> p k t", k=4),
                                   ACT.Copy).then_inc(gxhi, 1)

            def y_hi(job):
                act.wait_ge(units_done, job * FFN_UNITS + MOE0)
                for b in range(2):
                    act.activation(yhi[:, b * 512:(b + 1) * 512], ps[:, B_Y[0][b], :], ACT.Copy, scale=gate[:, 0:1])\
                        .then_inc(yhi_ready, 1)

            act.wait_ge(zero_set, 2)
            act.activation(put[:, :], zero[:, 0:SEQ].bitcast(F32), ACT.Copy).then_inc(put_now, 1)
            act.activation(gate[:, :], zero[:, 0:1].bitcast(F32), ACT.Copy).then_inc(put_now, 1)
            act.wait_ge(put_now, 2)
            act.wait_ge(y_clear, 1)
            act.wait_ge(table_ready, 1)
            n_jobs = act.value_load(jobs_i[0:1, 0:1], min_val=NE, max_val=JOBS)
            gather_out(0)
            with act.Fori(0, n_jobs) as job:
                r = job * STEPS
                for i in range(2):
                    cut(MOE0 + i, r)
                y_hi(job)
                for i in range(2, 6):
                    cut(MOE0 + i, r)
                glu_silu(0, r + EV_MOE, units_done, r * 6 + MOE0 + 4)
                act.wait_ge(sc_done, 4 * job + 4)
                act.wait_ge(put_out, 2 * job + 2)
                act.activation(put[:, :], put_next[:, :], ACT.Copy).then_inc(put_now, 1)
                act.activation(gate[:, :], gate_next[:, :], ACT.Copy).then_inc(put_now, 1)
                glu_thi(0, r + EV_MOE, r * 6 + MOE0 + 4)
                with act.Fori(1, STEPS) as s:
                    rs = job * STEPS + s
                    for i in range(4):
                        cut(MOE0 + i, rs)
                    glu_silu(0, rs + EV_MOE, units_done, rs * 6 + MOE0 + 2)
                    for i in range(2):
                        cut(MOE0 + 4 + i, rs)
                    glu_thi(0, rs + EV_MOE, rs * 6 + MOE0 + 4)
                gather_out(job + 1)
            y_hi(n_jobs)
            act.wait_ge(h_added, 4 * n_jobs + 4)
            norm_sums(5, h)

        @block.vector
        def _(dve):
            nxt = [0]
            chain = [0]

            def link(ins):
                chain[0] += 1
                ins.then_inc(dve_chain, 1)
                dve.wait_ge(dve_chain, chain[0])

            def cut(c, rounds):
                dve.wait_ge(hi_ready, c + RAW * rounds + 1)
                n = span(c)
                dve.tensor_tensor(wlo[:, c % CUT, 0:n], raw[:, c % RAW, 0:n], whi[:, c % CUT, 0:n].bitcast(F32),
                                  ALU.subtract).then_inc(lo_ready, 1)

            def cut_upto(n):
                while nxt[0] < n:
                    cut(nxt[0], 0)
                    nxt[0] += 1

            def norm(k, src):
                dve.wait_ge(std_done, k + 1)
                dve.reciprocal(rstd[:, 2 * k:2 * k + 2], std[:, 2 * k:2 * k + 2]).then_inc(rstd_done, 1)
                dve.wait_ge(rstd_done, k + 1)
                dve.wait_ge(gain_in[k % 2], 16 * (k // 2 + 1))
                for t in range(TILES):
                    dve.scalar_tensor_tensor(hn[:, t, :], src[:, t, :], rstd[:, 2 * k + t:2 * k + t + 1],
                                             gain[:, k % 2, :], ALU.mult, ALU.mult).then_inc(hn_done, 1)

            def xT_lo(op):
                for b in range(TR_BANKS[op]):
                    dve.wait_ge(xhi_ready, TR0[op] + b + 1)
                    dve.tensor_tensor(xlo[:, 2 * b:2 * b + 2, :], ps[:, b, :].rearrange("p (k t) -> p k t", k=2),
                                      xhi[:, 2 * b:2 * b + 2, :].bitcast(F32), ALU.subtract).then_inc(xlo_ready, 1)

            def chunk_out(c, dst):
                cut_upto(FIRST[c] + CHUNKS[c][2] // 4 + 2)
                dve.wait_ge(units_done, FIRST[c] + CHUNKS[c][2] // 4)
                dve.tensor_copy(dst, ps[:, 5 + 2 * (c % 2), 0:CHUNKS[c][1]]).then_inc(ev_dve, 1)

            def chunk_add(c):
                cut_upto(min(FIRST[c] + CHUNKS[c][2] // 4 + 2, MOE0 if c >= C_DO else FFN0 + 2))
                cols = slice(CHUNKS[c][3], CHUNKS[c][3] + 512)
                for t in range(TILES):
                    if t == 0:
                        dve.wait_ge(chunk_done, c + 1)
                    else:
                        dve.wait_ge(units_done, FIRST[c] + CHUNKS[c][2] // 4)
                    dve.tensor_tensor(h[:, t, cols], h[:, t, cols], ps[:, 4 + 2 * (c % 2) + t, :], ALU.add)\
                        .then_inc(ev_dve, 1)

            nm = sm[:, 32:64].rearrange("p (q i) -> p q i", q=2)
            den = sm[:, 64:96].rearrange("p (q i) -> p q i", q=2)
            wts = sm[:, 96:128].rearrange("p (q i) -> p q i", q=2)

            def attention(layer):
                base = ITEMS * layer
                for n in range(1, ITEMS + 3):
                    i = n - 1
                    if i < ITEMS:
                        dve.wait_ge(s_done, base + i + 1)
                        bank = 3 + (base + i) % 3
                        w0 = P if i < NH else SEQ
                        for qb, (a, b) in enumerate([(0, w0), (w0, w0 + SEQ)]):
                            dve.tensor_reduce(sm[:, 16 * qb + i:16 * qb + i + 1], ps[:, bank, a:b], AX.X, ALU.max,
                                              negate=True).then_inc(nmr_done, 1)
                        dve.wait_ge(nmr_done, 2 * (base + i + 1))
                        dve.tensor_scalar(free(sm[:, 32 + i:33 + i], (16, 2)), free(sm[:, i:i + 1], (16, 2)), 0.125,
                                          None, ALU.mult).then_inc(nm_ready, 1)
                    i = n - 2
                    if 0 <= i < ITEMS:
                        dve.wait_ge(pT_done, base + i + 1)
                        wait(dve, o_done, base + i - 1)
                        w = 384 if i < NH else 512
                        dve.tensor_copy(probsT[:, i % 2, 0:w], ps[:, 1 + (base + i) % 2, 0:w]).then_inc(pT_ready, 1)
                    if n in (6, 10, 14):
                        heads_out(layer, (n - 6) // 4)
                heads_out(layer, 3)

            def heads_out(layer, g):
                n = 4 * layer + g
                dve.wait_ge(o_done, 4 * (n + 1))
                dve.tensor_copy(oraw[:, :, 4 * g:4 * g + 4, :].rearrange("p q i d -> p q (i d)"),
                                ps[:, 6 + n % 2, :].rearrange("p (q c) -> p q c", q=2)).then_inc(o_out, 1)

            def combine0():
                f = sm[:, 128:152].rearrange("p (q i) -> p q i", q=2)
                es = sm[:, 152:176].rearrange("p (q i) -> p q i", q=2)
                nm2 = sm[:, 176:200].rearrange("p (q i) -> p q i", q=2)
                tmp = sm[:, 200:224].rearrange("p (q i) -> p q i", q=2)
                sink2 = free(sm[:, 256:257], (0, 2), (1, NH))
                dve.wait_ge(sink_in, 16)
                link(dve.tensor_scalar(sm[:, 256:268], sm[:, 496:508], -1.0, None, ALU.mult))
                link(dve.tensor_tensor(nm2, nm[:, :, 0:NH], sink2, ALU.min))
                dve.tensor_tensor(f, nm2, nm[:, :, 0:NH], ALU.subtract)
                dve.tensor_tensor(es, nm2, sink2, ALU.subtract).then_inc(fexp_in, 1)
                dve.wait_ge(fexp_out, 1)
                link(dve.tensor_tensor(tmp, f, den[:, :, 0:NH], ALU.mult))
                link(dve.tensor_tensor(tmp, tmp, es, ALU.add))
                link(dve.reciprocal(tmp, tmp))
                dve.tensor_tensor(wts[:, :, 0:NH], f, tmp, ALU.mult)
                link(dve.reciprocal(wts[:, :, NH:], den[:, :, NH:]))
                for t in range(TILES):
                    dve.tensor_tensor(hn[:, t, :].rearrange("p (i d) -> p i d", i=ITEMS), oraw[:, t, :, :],
                                      free(sm[:, 96 + 16 * t:97 + 16 * t], (1, ITEMS), (0, HD)), ALU.mult)\
                        .then_inc(cat_done, 1)

            def combine1():
                f = sm[:, 128:152].rearrange("p (q g i) -> p q g i", q=2, g=3)
                low = sm[:, 176:184].rearrange("p (q i) -> p q i", q=2)
                tmp = sm[:, 200:224].rearrange("p (q g i) -> p q g i", q=2, g=3)
                tot = sm[:, 184:192].rearrange("p (q i) -> p q i", q=2)
                link(dve.tensor_tensor(low, nm[:, :, 0:4], nm[:, :, 4:8], ALU.min))
                link(dve.tensor_tensor(low, low, nm[:, :, 8:12], ALU.min))
                for g in range(3):
                    last = dve.tensor_tensor(f[:, :, g, :], low, nm[:, :, 4 * g:4 * g + 4], ALU.subtract)
                last.then_inc(fexp_in, 1)
                dve.wait_ge(fexp_out, 2)
                link(dve.tensor_tensor(sm[:, 200:224].rearrange("p (q i) -> p q i", q=2),
                                       sm[:, 128:152].rearrange("p (q i) -> p q i", q=2), den[:, :, 0:NH], ALU.mult))
                link(dve.tensor_tensor(tot, tmp[:, :, 0, :], tmp[:, :, 1, :], ALU.add))
                link(dve.tensor_tensor(tot, tot, tmp[:, :, 2, :], ALU.add))
                link(dve.reciprocal(tot, tot))
                for g in range(3):
                    dve.tensor_tensor(wts[:, :, 4 * g:4 * g + 4], f[:, :, g, :], tot, ALU.mult)
                link(dve.reciprocal(wts[:, :, NH:], den[:, :, NH:]))
                half = NH * HD
                for t in range(TILES):
                    link(dve.tensor_tensor(oraw[:, t, 0:NH, :], oraw[:, t, 0:NH, :],
                                           free(sm[:, 96 + 16 * t:97 + 16 * t], (1, NH), (0, HD)), ALU.mult))
                    o = oraw[:, t, :, :].rearrange("p i d -> p (i d)")
                    link(dve.tensor_tensor(hn[:, t, 0:256], o[:, 0:256], o[:, 256:512], ALU.add))
                    dve.tensor_tensor(hn[:, t, 0:256], hn[:, t, 0:256], o[:, 512:half], ALU.add)
                    dve.tensor_tensor(hn[:, t, 256:512].rearrange("p (i d) -> p i d", i=MH), oraw[:, t, NH:, :],
                                      free(sm[:, 108 + 16 * t:109 + 16 * t], (1, MH), (0, HD)), ALU.mult)\
                        .then_inc(cat_done, 1)

            def glu_mul(t, ev):
                dve.wait_ge(silu_ready, ev + 1)
                dve.tensor_tensor(act_h[:, t, :], ps[:, B_U[t], :], silu[:, t, :], ALU.mult).then_inc(act_ready, 1)

            def glu_tlo(t, ev):
                dve.wait_ge(thi_ready, ev + 1)
                dve.tensor_tensor(tlo[:, :, t * P:(t + 1) * P], ps[:, B_G[t], :].rearrange("p (k t) -> p k t", k=FT),
                                  thi[:, :, t * P:(t + 1) * P].bitcast(F32), ALU.subtract).then_inc(tlo_ready, 1)

            dve.memset(table[32:33, :], 1.0).then_inc(table_one, 1)
            norm(0, hn)
            cut_upto(2)
            xT_lo(T_MEM)
            chunk_out(0, memkv[:, 0, 1, :])
            chunk_out(1, memkv[:, 1, 1, :])
            norm(1, h)
            xT_lo(T_MIX0)
            dve.wait_ge(rows_out, 64)
            for c in range(C_SI, C_SO):
                chunk_out(c, proj[:, 1, CHUNKS[c][3]:CHUNKS[c][3] + CHUNKS[c][1]])
            attention(0)
            combine0()
            xT_lo(T_CAT0)
            for c in (C_SO, C_SO + 1):
                chunk_add(c)
            norm(2, h)
            xT_lo(T_FFN0)
            dve.memset(zero[:, :].bitcast(F32), 0.0).then_inc(zero_set, 1)
            for i in range(4):
                cut(FFN0 + 2 + i, 0)
            for t in range(TILES):
                glu_mul(t, t)
            for t in range(TILES):
                glu_tlo(t, t)
            with dve.Fori(1, STEPS) as s:
                for i in range(4):
                    cut(FFN0 + i, s)
                for t in range(TILES):
                    glu_mul(t, s * TILES + t)
                for i in range(2):
                    cut(FFN0 + 4 + i, s)
                for t in range(TILES):
                    glu_tlo(t, s * TILES + t)
            nxt[0] = FFN0 + FFN_UNITS
            cut_upto(FIRST[C_DI] + 2)
            dve.wait_ge(units_done, FFN0 + FFN_UNITS)
            for t in range(TILES):
                for b in range(2):
                    dve.tensor_tensor(h[:, t, b * 512:(b + 1) * 512], h[:, t, b * 512:(b + 1) * 512],
                                      ps[:, B_Y[t][b], :], ALU.add).then_inc(ffn_added, 1)
            norm(3, h)
            xT_lo(T_MIX1)
            for c in range(C_DI, C_DO):
                chunk_out(c, proj[:, 1, CHUNKS[c][3]:CHUNKS[c][3] + CHUNKS[c][1]])
            attention(1)
            combine1()
            xT_lo(T_CAT1)
            for c in (C_DO, C_DO + 1):
                chunk_add(c)
            norm(4, h)

            dve.memset(zero[:, :].bitcast(F32), 0.0).then_inc(zero_set, 1)
            dve.memset(pos[:, :, :], -1.0)
            link(dve.memset(comb[:, :, :], 0.0))
            for t in range(TILES):
                dve.wait_ge(nhi_ready, t + 1)
                dve.tensor_tensor(nlo[:, t, :], hn[:, t, :], nhi[:, t, :].bitcast(F32), ALU.subtract)\
                    .then_inc(nlo_ready, 1)

            lg, d = rt[:, 0:16], rt[:, 16:32]
            l3 = lg.rearrange("p (t e) -> p t e", t=2)
            gt = rt[:, 32:160].rearrange("p (t e f) -> p t e f", t=2, e=NE)
            eq = rt[:, 192:320].rearrange("p (t e f) -> p t e f", t=2, e=NE)
            ex = rt[:, 160:176].rearrange("p (t e) -> p t e", t=2)
            rank, sel = rt[:, 320:336], rt[:, 336:352]
            top, tot = rt[:, 352:354], rt[:, 354:356]
            dve.wait_ge(logit_done, 1)
            link(dve.tensor_copy(lg, ps[:, 4, 0:16]))
            for t in range(TILES):
                other = free(rt[:, 8 * t:8 * t + 1], (0, NE), (1, NE))
                own = free(rt[:, 8 * t:8 * t + 1], (1, NE), (0, NE))
                dve.tensor_tensor(gt[:, t], other, own, ALU.is_gt)
                link(dve.tensor_tensor(eq[:, t], other, own, ALU.is_equal))
                link(dve.tensor_tensor(eq[:, t], eq[:, t], tri.rearrange("p (e f) -> p e f", e=NE), ALU.mult))
                link(dve.tensor_tensor(gt[:, t], gt[:, t], eq[:, t], ALU.add))
            dve.tensor_reduce(rank.rearrange("p (t e) -> p t e", t=2), gt, AX.X, ALU.add)
            link(dve.tensor_reduce(top, l3, AX.X, ALU.max))
            dve.tensor_scalar(sel, rank, 2.0, None, ALU.is_lt).then_inc(rank_in, 1)
            dve.tensor_tensor(ex, l3, free(top, (1, 2), (0, NE)), ALU.subtract).then_inc(top_in, 1)
            dve.wait_ge(top_exp, 1)
            dve.wait_ge(rank_in, 1)
            sel3 = sel.rearrange("p (t e) -> p t e", t=2)
            link(dve.tensor_tensor(ex, ex, sel3, ALU.mult))
            link(dve.tensor_reduce(tot, ex, AX.X, ALU.add))
            link(dve.reciprocal(tot, tot))
            link(dve.tensor_tensor(comb[:, :, 0:NE], ex, free(tot, (1, 2), (0, NE)), ALU.mult))
            dve.wait_ge(rank_done, 1)
            p1 = rt[:, 368:384].rearrange("p (t e) -> p t e", t=2)
            over = rt[:, 384:392]
            link(dve.scalar_tensor_tensor(rt[:, 368:384], ps[:, 5, 0:16], 1.0, sel, ALU.add, ALU.mult))
            dve.tensor_scalar(pos[:, :, 0:NE], p1, -1.0, None, ALU.add)
            link(dve.tensor_scalar(over, ps[:, 5, 16:24], float(P), None, ALU.is_gt))
            om = rt[:, 400:464].rearrange("p (e f) -> p e f", e=NE)
            link(dve.tensor_tensor(om, free(over, (0, NE), (1, NE)), tri.rearrange("p (e f) -> p e f", e=NE), ALU.mult))
            link(dve.tensor_reduce(rt[:, 392:400], om, AX.X, ALU.add))
            oh = rt[:, 464:464 + NE * MAX_OVER]
            for o in range(MAX_OVER):
                last = dve.scalar_tensor_tensor(oh[:, NE * o:NE * o + NE], rt[:, 392:400], float(o), over,
                                                ALU.is_equal, ALU.mult)
            link(last)
            oh3 = oh.rearrange("p (o e) -> p o e", e=NE)
            pr = rt[:, 512:512 + NE * MAX_OVER].rearrange("p (o e) -> p o e", e=NE)
            red = rt[:, 560:560 + MAX_OVER]
            for t in range(TILES):
                link(dve.tensor_tensor(pr, oh3, free(rt[:, 368 + 8 * t:369 + 8 * t], (0, MAX_OVER), (1, NE)), ALU.mult))
                link(dve.tensor_reduce(red, pr, AX.X, ALU.add))
                link(dve.tensor_scalar(pos[:, t, NE:JOBS], red, -1.0 - P, None, ALU.add))
                link(dve.tensor_tensor(pr, oh3, free(comb[:, t, 0:1], (0, MAX_OVER), (1, NE)), ALU.mult))
                link(dve.tensor_reduce(comb[:, t, NE:JOBS], pr, AX.X, ALU.add))
            link(dve.tensor_tensor(pr, oh3, free(expert_no, (0, MAX_OVER), (1, NE)), ALU.mult))
            dve.tensor_reduce(rt[:, 570:570 + MAX_OVER], pr, AX.X, ALU.add)
            link(dve.tensor_reduce(rt[:, 569:570], over, AX.X, ALU.add))
            link(dve.tensor_scalar(rt[:, 568:569], rt[:, 569:570], float(NE), None, ALU.add))
            dve.tensor_copy(jobs_i[0:1, 0:2 + MAX_OVER], rt[0:1, 568:570 + MAX_OVER]).then_inc(table_ready, 1)

            def build_pick(q):
                wait(dve, put_done, q)
                for t in range(TILES):
                    dve.tensor_scalar(pick[:, t, :], iota, pos[:, t, bass.ds(q, 1)], None, ALU.is_equal)\
                        .then_inc(pick_ready, 1)

            def gather_lo(q):
                for b in range(2):
                    dve.wait_ge(gxhi, 2 * q + b + 1)
                    dve.tensor_tensor(xlo[:, 4 * b:4 * b + 4, 0:P], ps[:, B_X[b], :].rearrange("p (k t) -> p k t", k=4),
                                      xhi[:, 4 * b:4 * b + 4, 0:P].bitcast(F32), ALU.subtract).then_inc(gxlo, 1)

            def y_lo(job):
                for b in range(2):
                    dve.wait_ge(yhi_ready, 2 * job + b + 1)
                    dve.scalar_tensor_tensor(ylo[:, b * 512:(b + 1) * 512], ps[:, B_Y[0][b], :], gate[:, 0:1],
                                             yhi[:, b * 512:(b + 1) * 512].bitcast(F32), ALU.mult, ALU.subtract)\
                        .then_inc(ylo_ready, 1)

            def add_scattered(job):
                for n in range(4):
                    dve.wait_ge(sc_done, 4 * job + n + 1)
                    t, b = n // 2, n % 2
                    dve.tensor_tensor(h[:, t, b * 512:(b + 1) * 512], h[:, t, b * 512:(b + 1) * 512],
                                      ps[:, B_SC[n], :], ALU.add).then_inc(h_added, 1)

            for t in range(TILES):
                dve.tensor_scalar(pick[:, t, :], iota, pos[:, t, 0:1], None, ALU.is_equal).then_inc(pick_ready, 1)
            dve.wait_ge(table_ready, 1)
            n_jobs = dve.value_load(jobs_i[0:1, 0:1], min_val=NE, max_val=JOBS)
            gather_lo(0)
            with dve.Fori(0, n_jobs) as job:
                r = job * STEPS
                for i in range(2):
                    cut(MOE0 + i, r)
                y_lo(job)
                build_pick(job + 1)
                for i in range(2, 6):
                    cut(MOE0 + i, r)
                glu_mul(0, r + EV_MOE)
                add_scattered(job)
                glu_tlo(0, r + EV_MOE)
                with dve.Fori(1, STEPS) as s:
                    rs = job * STEPS + s
                    for i in range(4):
                        cut(MOE0 + i, rs)
                    glu_mul(0, rs + EV_MOE)
                    for i in range(2):
                        cut(MOE0 + 4 + i, rs)
                    glu_tlo(0, rs + EV_MOE)
                gather_lo(job + 1)
            y_lo(n_jobs)
            add_scattered(n_jobs)
            norm(5, h)

        @block.tensor
        def _(pe):
            def three(dst, ahi, alo, bhi, blo, start, stop):
                pe.matmul(dst, ahi, bhi, start=start, stop=False)
                pe.matmul(dst, ahi, blo, start=False, stop=False)
                return pe.matmul(dst, alo, bhi, start=False, stop=stop)

            def transpose_x(op):
                for b in range(TR_BANKS[op]):
                    for j in range(4):
                        kt, t = 2 * b + j // 2, j % 2
                        last = pe.transpose(ps[:, b, j * P:(j + 1) * P], hn[:, t, kt * P:(kt + 1) * P], ident)
                    last.then_inc(tr_done, 1)

            def chunk(c):
                _, width, rows_, _ = CHUNKS[c]
                if c >= 2:
                    pe.wait_ge(ev_act, ACT_EV[c - 2])
                    pe.wait_ge(ev_dve, DVE_EV[c - 2])
                n_units = rows_ // 4
                for i in range(n_units):
                    u = FIRST[c] + i
                    pe.wait_ge(lo_ready, u + 1)
                    for t in range(TILES):
                        dst = ps[:, 4 + 2 * (c % 2) + t, 0:width]
                        for j in range(4):
                            kt = 4 * i + j
                            cols = slice(j * width, (j + 1) * width)
                            last = three(dst, xhi[:, kt, t * P:(t + 1) * P], xlo[:, kt, t * P:(t + 1) * P],
                                         whi[:, u % CUT, cols], wlo[:, u % CUT, cols],
                                         kt == 0, kt == 4 * n_units - 1)
                        if i == n_units - 1 and t == 0:
                            last.then_inc(chunk_done, 1)
                    last.then_inc(units_done, 1)

            def attention(layer):
                base = ITEMS * layer
                for n in range(ITEMS + 3):
                    if n < ITEMS:
                        q, k, _ = items[layer][n]
                        wait(pe, qk_ready, base + n)
                        for t in range(TILES):
                            pe.transpose(ps[0:HD, 0, t * P:(t + 1) * P], proj[:, t, q:q + HD], ident)
                        for t in range(TILES):
                            last = pe.transpose(ps[0:HD, 0, SEQ + t * P:SEQ + (t + 1) * P], kv(layer, n, t, k), ident)
                        last.then_inc(qkT_done, 1)
                    i = n - 1
                    if 0 <= i < ITEMS:
                        pe.wait_ge(qk_ready, base + i + 1)
                        wait(pe, p_ready, 2 * (base + i - 2))
                        if i == 0:
                            pe.wait_ge(bias_in, 48 * (layer + 1))
                        bank = 3 + (base + i) % 3
                        w0 = P if i < NH else SEQ
                        for qb in range(TILES):
                            nk = w0 if qb == 0 else SEQ
                            dst = ps[:, bank, qb * w0:qb * w0 + nk]
                            last = pe.matmul(dst, qk[:, i % 2, qb * P:(qb + 1) * P], qk[:, i % 2, SEQ:SEQ + nk],
                                             start=True, stop=i >= NH)
                            if i < NH:
                                last = pe.matmul(dst, anti, bias[:, i, SEQ - nk:SEQ], start=False, stop=True)
                        last.then_inc(s_done, 1)
                    i = n - 2
                    if 0 <= i < ITEMS:
                        pe.wait_ge(p_ready, 2 * (base + i + 1))
                        wait(pe, pT_ready, base + i - 1)
                        for j in range(3 if i < NH else 4):
                            last = pe.transpose(ps[:, 1 + (base + i) % 2, j * P:(j + 1) * P],
                                                probs[:, i % 2, j * P:(j + 1) * P], ident)
                        last.then_inc(pT_done, 1)
                    i = n - 3
                    if 0 <= i < ITEMS:
                        pe.wait_ge(pT_ready, base + i + 1)
                        wait(pe, o_out, (base + i) // 4 - 1)
                        v = items[layer][i][2]
                        blocks = [[0], [0, 1]] if i < NH else [[0, 1], [0, 1]]
                        j = 0
                        for qb in range(TILES):
                            for m in blocks[qb]:
                                c0 = qb * SEQ + i % 4 * HD
                                last = pe.matmul(ps[:, 6 + (base + i) // 4 % 2, c0:c0 + HD],
                                                 probsT[:, i % 2, j * P:(j + 1) * P], kv(layer, i, m, v),
                                                 start=m == 0, stop=m == blocks[qb][-1])
                                j += 1
                        last.then_inc(o_done, 1)

            def unit_in(c, rounds, tiles, bank, half, first_tile_done=None):
                pe.wait_ge(lo_ready, c + RAW * rounds + 1)
                for t in range(tiles):
                    for j in range(4):
                        kt = 4 * half + j
                        cols = slice(j * FCH, (j + 1) * FCH)
                        last = three(ps[:, bank[t], :], xhi[:, kt, t * P:(t + 1) * P], xlo[:, kt, t * P:(t + 1) * P],
                                     whi[:, c % CUT, cols], wlo[:, c % CUT, cols], kt == 0, kt == KT - 1)
                    if first_tile_done is not None and t == 0:
                        last.then_inc(first_tile_done, 1)
                last.then_inc(units_done, 1)

            def unit_out(c, rounds, tiles, half, final=False):
                pe.wait_ge(lo_ready, c + RAW * rounds + 1)
                for t in range(tiles):
                    for j in range(2):
                        ft = 2 * half + j
                        for b in range(2):
                            cols = slice(j * D + b * 512, j * D + b * 512 + 512)
                            last = three(ps[:, B_Y[t][b], :], thi[:, ft, t * P:(t + 1) * P],
                                         tlo[:, ft, t * P:(t + 1) * P], whi[:, c % CUT, cols], wlo[:, c % CUT, cols],
                                         False, final and half == 1 and j == 1)
                last.then_inc(units_done, 1)

            def hidden_t(t, ev):
                pe.wait_ge(act_ready, ev + 1)
                for j in range(FT):
                    last = pe.transpose(ps[:, B_G[t], j * P:(j + 1) * P], act_h[:, t, j * P:(j + 1) * P], ident)
                last.then_inc(t_done, 1)

            def products_in(c, rounds, tiles, ev=None):
                for i in range(2):
                    unit_in(c + i, rounds, tiles, B_U, i)
                if ev is not None:
                    pe.wait_ge(tlo_ready, ev)
                unit_in(c + 2, rounds, tiles, B_G, 0)
                unit_in(c + 3, rounds, tiles, B_G, 1, g_done if tiles > 1 else None)

            def clear_y(tiles, stop=False):
                for t in range(tiles):
                    for b in range(2):
                        last = pe.matmul(ps[:, B_Y[t][b], :], zero[:, 0:P], zero[:, :], start=True, stop=stop)
                return last

            pe.wait_ge(onehot_in, 16)
            pe.wait_ge(table_in, 16)
            pe.wait_ge(table_one, 1)
            for g in range(4):
                n = NH if g == 0 else 4
                heads = table[:, 0:NH] if g == 0 else table[:, 4 * g - 4:4 * g]
                last = pe.matmul(ps[0:n, g, 0:RLEN], heads, onehot[:, g, :], start=True, stop=True)
            last.then_inc(rows_mm, 1)
            pe.wait_ge(const_in, 16)
            pe.wait_ge(rows_sb, 4)
            pe.wait_ge(hn_done, 2)
            transpose_x(T_MEM)
            pe.wait_ge(xlo_ready, TR0[T_MEM + 1])
            chunk(0)
            chunk(1)
            pe.wait_ge(hn_done, 4)
            transpose_x(T_MIX0)
            pe.wait_ge(xlo_ready, TR0[T_MIX0 + 1])
            for c in range(C_SI, C_SO):
                chunk(c)
            pe.wait_ge(ev_act, ACT_EV[C_SO - 1])
            pe.wait_ge(ev_dve, DVE_EV[C_SO - 1])
            attention(0)
            pe.wait_ge(cat_done, 2)
            transpose_x(T_CAT0)
            pe.wait_ge(xlo_ready, TR0[T_CAT0 + 1])
            chunk(C_SO)
            chunk(C_SO + 1)
            pe.wait_ge(hn_done, 6)
            transpose_x(T_FFN0)
            pe.wait_ge(xlo_ready, TR0[T_FFN0 + 1])
            products_in(FFN0, 0, TILES)
            pe.wait_ge(zero_set, 1)
            clear_y(TILES)
            for t in range(TILES):
                hidden_t(t, t)
            with pe.Fori(1, STEPS) as s:
                products_in(FFN0 - 2, s, TILES, s * TILES)
                unit_out(FFN0 + 2, s, TILES, 0)
                for t in range(TILES):
                    hidden_t(t, s * TILES + t)
                unit_out(FFN0 + 3, s, TILES, 1)
            pe.wait_ge(tlo_ready, EV_MOE)
            for i in range(2):
                unit_out(FFN0 + FFN_UNITS - 2 + i, 0, TILES, i, True)
            pe.wait_ge(hn_done, 8)
            transpose_x(T_MIX1)
            pe.wait_ge(xlo_ready, TR0[T_MIX1 + 1])
            for c in range(C_DI, C_DO):
                chunk(c)
            pe.wait_ge(ev_act, ACT_EV[C_DO - 1])
            pe.wait_ge(ev_dve, DVE_EV[C_DO - 1])
            attention(1)
            pe.wait_ge(cat_done, 4)
            transpose_x(T_CAT1)
            pe.wait_ge(xlo_ready, TR0[T_CAT1 + 1])
            chunk(C_DO)
            chunk(C_DO + 1)
            pe.wait_ge(hn_done, 10)
            transpose_x(T_ROUTE)
            pe.wait_ge(xtf_ready, 4)
            pe.wait_ge(rw_in, 16)
            for t in range(TILES):
                for kt in range(KT):
                    last = pe.matmul(ps[:, 4, t * NE:(t + 1) * NE], xtf[:, kt, t * P:(t + 1) * P], rw[:, kt, :],
                                     start=kt == 0, stop=kt == KT - 1)
            last.then_inc(logit_done, 1)
            pe.wait_ge(rank_in, 1)
            sel = [rt[:, 336 + NE * t:336 + NE * (t + 1)] for t in range(TILES)]
            pe.matmul(ps[:, 5, 0:NE], before, sel[0], start=True, stop=True)
            pe.matmul(ps[:, 5, NE:2 * NE], ones, sel[0], start=True, stop=False)
            pe.matmul(ps[:, 5, NE:2 * NE], before, sel[1], start=False, stop=True)
            pe.matmul(ps[:, 5, 2 * NE:3 * NE], ones, sel[0], start=True, stop=False)
            pe.matmul(ps[:, 5, 2 * NE:3 * NE], ones, sel[1], start=False, stop=True).then_inc(rank_done, 1)

            def gather(q):
                pe.wait_ge(pick_ready, 2 * q + 2)
                for kt in range(KT):
                    dst = ps[:, B_X[kt // 4], kt % 4 * P:(kt % 4 + 1) * P]
                    for n, (t, part) in enumerate([(t, part) for t in range(TILES) for part in (nhi, nlo)]):
                        last = pe.matmul(dst, part[:, t, kt * P:(kt + 1) * P], pick[:, t, :], start=n == 0, stop=n == 3)
                    if kt % 4 == 3:
                        last.then_inc(gx_done, 1)
                for t in range(TILES):
                    pe.transpose(ps[:, B_PUT, t * P:(t + 1) * P], pick[:, t, :].bitcast(F32), ident)
                for t in range(TILES):
                    last = pe.matmul(ps[:, B_PUT, SEQ:SEQ + 1], pick[:, t, :].bitcast(F32), comb[:, t, bass.ds(q, 1)],
                                     start=t == 0, stop=t == 1)
                last.then_inc(put_done, 1)

            def scatter(job):
                pe.wait_ge(put_now, 2 * job + 2)
                pe.wait_ge(ylo_ready, 2 * job + 2)
                pe.wait_ge(put_out, 2 * job + 2)
                for n in range(4):
                    t, b = n // 2, n % 2
                    pe.matmul(ps[:, B_SC[n], :], put[:, t * P:(t + 1) * P], yhi[:, b * 512:(b + 1) * 512],
                              start=True, stop=False)
                    pe.matmul(ps[:, B_SC[n], :], put[:, t * P:(t + 1) * P], ylo[:, b * 512:(b + 1) * 512],
                              start=False, stop=True).then_inc(sc_done, 1)

            pe.wait_ge(table_ready, 1)
            pe.wait_ge(nlo_ready, 2)
            pe.wait_ge(zero_set, 2)
            clear_y(1, True).then_inc(y_clear, 1)
            n_jobs = pe.value_load(jobs_i[0:1, 0:1], min_val=NE, max_val=JOBS)
            gather(0)
            with pe.Fori(0, n_jobs) as job:
                r = job * STEPS
                pe.wait_ge(gxlo, 2 * job + 2)
                products_in(MOE0, r, 1)
                scatter(job)
                clear_y(1)
                hidden_t(0, r + EV_MOE)
                with pe.Fori(1, STEPS) as s:
                    rs = job * STEPS + s
                    products_in(MOE0 - 2, rs, 1, rs + EV_MOE)
                    unit_out(MOE0 + 2, rs, 1, 0)
                    hidden_t(0, rs + EV_MOE)
                    unit_out(MOE0 + 3, rs, 1, 1)
                pe.wait_ge(h_added, 4 * job + 4)
                gather(job + 1)
                pe.wait_ge(tlo_ready, r + EV_MOE + STEPS)
                for i in range(2):
                    unit_out(MOE0 + FFN_UNITS - 2 + i, r, 1, i, True)
            pe.wait_ge(gxlo, 2 * n_jobs + 2)
            scatter(n_jobs)


_INS = ["x", "mem", "rel_bias_table", "mem_norm", "norm_mix", "norm_ffn", "final_norm", "swa_w_in", "swa_sinks",
        "swa_w_mem_kv", "swa_w_out", "dil_w_in", "dil_w_mem_kv", "dil_w_out", "ffn_gate", "ffn_up", "ffn_down",
        "router", "moe_gate", "moe_up", "moe_down"]


def kernel(**inputs):
    import concourse.bacc as bacc
    from concourse.bass_utils import run_bass_kernel_spmd

    nc = bacc.Bacc("TRN2", target_bir_lowering=False, num_devices=1)
    index_mats, bias_onehot = shape_constants()
    arrays = {name: np.ascontiguousarray(inputs[name]) for name in _INS}
    arrays["index_mats"], arrays["bias_onehot"] = index_mats, bias_onehot
    args = [nc.dram_tensor(f"in_{name}", a.shape, mybir.dt.from_np(a.dtype), kind="ExternalInput").ap()
            for name, a in arrays.items()]
    out = nc.dram_tensor("out_trunk", (1, SEQ, D), F32, kind="ExternalOutput").ap()
    trunk(nc, *args, out)
    result = run_bass_kernel_spmd(nc, [{f"in_{name}": a for name, a in arrays.items()}], core_ids=[0])
    return result.results[0]["out_trunk"]
```

```python
from contextlib import ExitStack

import numpy as np

import concourse.bass as bass
from concourse import mybir

F32 = mybir.dt.float32
F32R = mybir.dt.float32r
I32 = mybir.dt.int32
ACT = mybir.ActivationFunctionType
ALU = mybir.AluOpType
AX = mybir.AxisListType

P = 128
D = 1024
SEQ = 256
TILES = SEQ // P
KT = D // P
DFF = 3584
FCH = 512
STEPS = DFF // FCH
FT = FCH // P
NE = 8
HD = 64
NH = 12
MH = 4
ITEMS = NH + MH
NEG = -1e30
EPS = 1e-5
RAW = 6
CUT = 3
UNIT = 2048
SWA_IN = 1408
DIL_IN = 2560
MAX_OVER = (2 * SEQ) // (P + 1)
JOBS = NE + MAX_OVER
COLS = JOBS + 1
RLEN = 3 * P

CHUNKS = (
    [("mk0", 512, 8, 0), ("mk1", 512, 8, 0)]
    + [("si", min(512, SWA_IN - o), 8, o) for o in range(0, SWA_IN, 512)]
    + [("so", 512, 8, o) for o in range(0, D, 512)]
    + [("di", 512, 8, o) for o in range(0, DIL_IN, 512)]
    + [("do", 512, 4, o) for o in range(0, D, 512)]
)
FFN_UNITS = STEPS * 6


def plan_units():
    first, n, ffn = [], 0, None
    for name, _, rows, _ in CHUNKS:
        if name == "di" and ffn is None:
            ffn, n = n, n + FFN_UNITS
        first.append(n)
        n += rows // 4
    return first, ffn, n


FIRST, FFN0, MOE0 = plan_units()
C_SI, C_SO, C_DI, C_DO = 2, 5, 7, 12
ACT_EV = [sum(CHUNKS[i][0] not in ("so", "do") for i in range(c + 1)) for c in range(len(CHUNKS))]
DVE_EV = [sum(2 if CHUNKS[i][0] in ("so", "do") else 1 for i in range(c + 1)) for c in range(len(CHUNKS))]
TR_BANKS = [4, 4, 4, 4, 4, 2, 4]
TR0 = [sum(TR_BANKS[:i]) for i in range(len(TR_BANKS) + 1)]
T_MEM, T_MIX0, T_CAT0, T_FFN0, T_MIX1, T_CAT1, T_ROUTE = range(7)
XT_FREE = [0, FIRST[C_SI], FIRST[C_SO], FFN0, FIRST[C_DI], FIRST[C_DO]]
EV_MOE = TILES * STEPS


def t5_bucket(dist):
    d = np.maximum(dist, 0)
    ratio = np.maximum(d, 1).astype(np.float32) / np.float32(16)
    large = 16 + (np.log(ratio).astype(np.float32) / np.float32(np.log(2048 / 16)) * 16).astype(np.int32)
    return np.where(d < 16, d, np.minimum(large, 31))


def shape_constants():
    c = np.zeros((P, 5 * P + 80), np.float32)
    i = np.arange(P)
    c[:, 0:P] = np.eye(P)
    c[:, P:2 * P] = np.eye(P)[::-1]
    c[:, 2 * P:3 * P] = i[:, None] < i[None, :]
    c[:, 3 * P:4 * P] = 1.0
    c[:, 4 * P:5 * P] = i[None, :]
    e = np.arange(NE)
    c[:, 5 * P:5 * P + 64] = (e[None, :] < e[:, None]).reshape(-1)
    c[:, 5 * P + 64] = EPS
    c[:, 5 * P + 65:5 * P + 73] = e
    dist = 2 * P - 1 - np.arange(RLEN)
    one = np.zeros((33, 4, RLEN), np.float32)
    b = t5_bucket(dist)
    for g, (most, dil) in enumerate([(127, 1), (128, 1), (512, 4), (2048, 16)]):
        one[b, g, np.arange(RLEN)] = 1.0
        ok = (dist >= 0) & (dist <= most) & (dist % dil == 0)
        one[32, g] = np.where(ok, 0.0, NEG)
    return c, one


def wait(eng, sem, value):
    if not isinstance(value, int) or value > 0:
        eng.wait_ge(sem, value)


def free(ap, *dims):
    return bass.AP(ap.tensor, ap.offset, [list(ap.ap[0])] + [list(d) for d in dims])


def trunk(nc, x, mem, rel_bias_table, mem_norm, norm_mix, norm_ffn, final_norm, swa_w_in, swa_sinks,
          swa_w_mem_kv, swa_w_out, dil_w_in, dil_w_mem_kv, dil_w_out, ffn_gate, ffn_up, ffn_down, router,
          moe_gate, moe_up, moe_down, index_mats, bias_onehot, out):
    chunk_w = {
        "mk0": swa_w_mem_kv, "mk1": dil_w_mem_kv, "si": swa_w_in, "so": swa_w_out, "di": dil_w_in, "do": dil_w_out,
    }
    chunk_w = {k: v.rearrange("z (k p) f -> p (z k) f", p=P) for k, v in chunk_w.items()}
    ffn_in = [w.rearrange("z (k p) f -> p (z k) f", p=P) for w in (ffn_up, ffn_gate)]
    ffn_out = ffn_down.rearrange("z (k p) f -> p (z k) f", p=P)
    moe_in = [w.rearrange("z e (k p) f -> p (z e) k f", p=P) for w in (moe_up, moe_gate)]
    moe_out = moe_down.rearrange("z e (k p) f -> p (z e) k f", p=P)
    gains = [mem_norm, norm_mix[0, :], norm_ffn[0, :], norm_mix[1, :], norm_ffn[1, :], final_norm]

    bias_rows = [nc.dram_tensor(f"bias_rows_{i}", (NH, RLEN), F32, kind="Internal").ap() for i in range(2)]

    ctx = ExitStack()
    with ctx:
        def sb(name, shape, dt=F32, scope=ctx):
            return scope.enter_context(nc.sbuf_tensor(name, shape, dt))

        def sem(name):
            return ctx.enter_context(nc.semaphore(name))

        raw = sb("raw", [P, RAW, UNIT])
        whi = sb("whi", [P, CUT, UNIT], F32R)
        wlo = sb("wlo", [P, CUT, UNIT], F32R)
        h = sb("h", [P, TILES, D])
        hn = sb("hn", [P, TILES, D])
        xhi = sb("xhi", [P, KT, SEQ], F32R)
        xlo = sb("xlo", [P, KT, SEQ], F32R)
        gain = sb("gain", [P, 2, D])
        memkv = sb("memkv", [P, 2, TILES, 512])
        mats = sb("mats", [P, 5 * P + 80])
        stats = sb("stats", [P, 64])
        squares = sb("squares", [P, D])
        ident, anti, before, ones, iota = (mats[:, i * P:(i + 1) * P] for i in range(5))
        tri, eps, expert_no = mats[:, 640:704], mats[:, 704:705], mats[:, 705:713]
        ssq, std, rstd = stats[:, 0:12], stats[:, 16:28], stats[:, 32:44]

        with ExitStack() as mix:
            proj = sb("proj", [P, TILES, DIL_IN], scope=mix)
            bias = sb("bias", [P, NH, SEQ], scope=mix)
            qk = sb("qk", [HD, 2, 512], scope=mix)
            probs = sb("probs", [P, 2, 512], scope=mix)
            probsT = sb("probsT", [P, 2, 512], scope=mix)
            oraw = sb("oraw", [P, TILES, ITEMS, HD], scope=mix)
            sm = sb("sm", [P, 512], scope=mix)
        with ExitStack() as glu:
            thi = sb("thi", [P, FT, SEQ], F32R, scope=glu)
            tlo = sb("tlo", [P, FT, SEQ], F32R, scope=glu)
            silu = sb("silu", [P, TILES, FCH], scope=glu)
            act_h = sb("act_h", [P, TILES, FCH], scope=glu)
            nhi = sb("nhi", [P, TILES, D], F32R, scope=glu)
            nlo = sb("nlo", [P, TILES, D], F32R, scope=glu)
            yhi = sb("yhi", [P, D], F32R, scope=glu)
            ylo = sb("ylo", [P, D], F32R, scope=glu)
            zero = sb("zero", [P, 512], F32R, scope=glu)
            pick = sb("pick", [P, TILES, P], F32R, scope=glu)
            put_next = sb("put_next", [P, SEQ], scope=glu)
            put = sb("put", [P, SEQ], F32R, scope=glu)
            gate_next = sb("gate_next", [P, 1], scope=glu)
            gate = sb("gate", [P, 1], scope=glu)
            rt = sb("rt", [P, 1024], scope=glu)
            rw = sb("rw", [P, KT, NE], scope=glu)
            pos = sb("pos", [P, TILES, COLS], scope=glu)
            comb = sb("comb", [P, TILES, COLS], scope=glu)
            jobs_i = sb("jobs_i", [1, 8], I32, scope=glu)
        with ExitStack() as early:
            onehot = sb("onehot", [33, 4, RLEN], scope=early)
            table = sb("table", [33, NH], scope=early)
            rows = sb("rows", [NH, 4, RLEN], scope=early)
        xtf = memkv[:, :, :, :].rearrange("p l t c -> p (l t c)").rearrange("p (k t) -> p k t", k=KT)
        ps = ctx.enter_context(nc.psum_tensor("ps", [P, 8, 512], F32))

        mem_in, x_in, const_in, out_done = sem("mem_in"), sem("x_in"), sem("const_in"), sem("out_done")
        onehot_in, table_in, sink_in, rw_in = sem("onehot_in"), sem("table_in"), sem("sink_in"), sem("rw_in")
        gain_in = [sem("gain_in0"), sem("gain_in1")]
        raw_full = [sem(f"raw_full{i}") for i in range(RAW)]
        hi_ready, lo_ready, units_done = sem("hi_ready"), sem("lo_ready"), sem("units_done")
        table_one, rows_mm, rows_sb, rows_out, bias_in = (
            sem("table_one"), sem("rows_mm"), sem("rows_sb"), sem("rows_out"), sem("bias_in"))
        sq_done, std_done, rstd_done, hn_done = sem("sq_done"), sem("std_done"), sem("rstd_done"), sem("hn_done")
        tr_done, xhi_ready, xlo_ready = sem("tr_done"), sem("xhi_ready"), sem("xlo_ready")
        chunk_done, ev_act, ev_dve, y0_done = sem("chunk_done"), sem("ev_act"), sem("ev_dve"), sem("y0_done")
        qkT_done, qk_ready, s_done, nmr_done, nm_ready = (
            sem("qkT_done"), sem("qk_ready"), sem("s_done"), sem("nmr_done"), sem("nm_ready"))
        p_ready, pT_done, pT_ready, o_done, o_out = (
            sem("p_ready"), sem("pT_done"), sem("pT_ready"), sem("o_done"), sem("o_out"))
        fexp_in, fexp_out, cat_done = sem("fexp_in"), sem("fexp_out"), sem("cat_done")
        dve_chain = sem("dve_chain")
        g_done, silu_ready, act_ready, t_done, thi_ready, tlo_ready = (
            sem("g_done"), sem("silu_ready"), sem("act_ready"), sem("t_done"), sem("thi_ready"), sem("tlo_ready"))
        zero_set, ffn_added = sem("zero_set"), sem("ffn_added")
        xtf_ready, logit_done, top_in, top_exp, rank_in, rank_done, comb_ready, table_ready = (
            sem("xtf_ready"), sem("logit_done"), sem("top_in"), sem("top_exp"), sem("rank_in"), sem("rank_done"),
            sem("comb_ready"), sem("table_ready"))
        nhi_ready, nlo_ready = sem("nhi_ready"), sem("nlo_ready")
        pick_ready, gx_done, put_done, gxhi, gxlo, put_out, put_now = (
            sem("pick_ready"), sem("gx_done"), sem("put_done"), sem("gxhi"), sem("gxlo"), sem("put_out"),
            sem("put_now"))
        yhi_ready, ylo_ready, sc_done, h_added = sem("yhi_ready"), sem("ylo_ready"), sem("sc_done"), sem("h_added")
        block = ctx.enter_context(nc.Block())

        items = [[], []]
        for i in range(NH):
            items[0].append((i * HD, 768 + i // 4 * HD, 960 + i // 4 * HD))
            base = i // 4 * 768 + i % 4 * HD
            items[1].append((base, base + 256, base + 512))
        for m in range(MH):
            items[0].append((1152 + m * HD, m * HD, 256 + m * HD))
            items[1].append((2304 + m * HD, m * HD, 256 + m * HD))

        def kv(layer, i, t, col):
            src = proj[:, t, col:col + HD] if i < NH else memkv[:, layer, t, col:col + HD]
            return src

        B_U, B_G, B_Y = (0, 1), (2, 3), ((4, 5), (6, 7))
        B_X, B_PUT, B_SC = (6, 7), 3, (1, 3, 6, 7)
        B_LG, B_RANK = (4, 6), 5

        def uses(c, rounds):
            return c // RAW + 1 + rounds

        def token_banks(op, t):
            n = TR_BANKS[op] // TILES
            return [(t * n + i, i) for i in range(n)]

        def part(x3, half, t):
            return x3[:, 4 * half:4 * half + 4, t * P:(t + 1) * P]

        def four(bank):
            return ps[:, bank, :].rearrange("p (k t) -> p k t", k=4)

        def span(c):
            for k, (_, width, rows_, _) in enumerate(CHUNKS):
                if FIRST[k] <= c < FIRST[k] + rows_ // 4:
                    return 4 * width
            return UNIT

        @block.sync
        def _(sp):
            sp.dma_start(hn[:, :, :], mem[0].rearrange("(t p) d -> p t d", p=P)).then_inc(mem_in, 16)
            sp.dma_start(h[:, :, :], x[0].rearrange("(t p) d -> p t d", p=P)).then_inc(x_in, 16)

            def load(c, rounds, src):
                wait(sp, lo_ready, c + RAW * rounds - RAW + 1)
                dst = raw[:, c % RAW, 0:span(c)].rearrange("p (k f) -> p k f", k=src.shape[-2])
                sp.dma_start(dst, src).then_inc(raw_full[c % RAW], 16)

            def load_chunks(lo, hi):
                for k in range(lo, hi):
                    name, width, rows_, off = CHUNKS[k]
                    for i in range(rows_ // 4):
                        load(FIRST[k] + i, 0, chunk_w[name][:, 4 * i:4 * i + 4, off:off + width])

            load_chunks(0, C_DI)
            for i in range(4):
                load(FFN0 + i, 0, ffn_in[i // 2][:, i % 2 * 4:i % 2 * 4 + 4, 0:FCH])
            with sp.Fori(1, STEPS) as s:
                for i in range(4):
                    load(FFN0 - 2 + i, s, ffn_in[i // 2][:, i % 2 * 4:i % 2 * 4 + 4, bass.ds(s * FCH, FCH)])
                for i in range(2):
                    load(FFN0 + 2 + i, s, ffn_out[:, bass.ds(s * FT - FT + 2 * i, 2), :])
            for i in range(2):
                load(FFN0 + FFN_UNITS - 2 + i, 0, ffn_out[:, (STEPS - 1) * FT + 2 * i:(STEPS - 1) * FT + 2 * i + 2, :])
            load_chunks(C_DI, len(CHUNKS))

            def load_expert(job, e):
                for i in range(4):
                    load(MOE0 + i, STEPS * job, moe_in[i // 2][:, bass.ds(e, 1), i % 2 * 4:i % 2 * 4 + 4, 0:FCH])
                with sp.Fori(1, STEPS) as s:
                    for i in range(4):
                        load(MOE0 - 2 + i, job * STEPS + s,
                             moe_in[i // 2][:, bass.ds(e, 1), i % 2 * 4:i % 2 * 4 + 4, bass.ds(s * FCH, FCH)])
                    for i in range(2):
                        load(MOE0 + 2 + i, job * STEPS + s,
                             moe_out[:, bass.ds(e, 1), bass.ds(s * FT - FT + 2 * i, 2), :])
                for i in range(2):
                    f = (STEPS - 1) * FT + 2 * i
                    load(MOE0 + FFN_UNITS - 2 + i, STEPS * job, moe_out[:, bass.ds(e, 1), f:f + 2, :])

            with sp.Fori(0, NE) as job:
                load_expert(job, job)
            sp.wait_ge(table_ready, 1)
            n_over = sp.value_load(jobs_i[0:1, 1:2], min_val=0, max_val=MAX_OVER)
            with sp.If(n_over > 0):
                with sp.Fori(0, n_over) as o:
                    e = sp.value_load(jobs_i[0:1, bass.ds(o + 2, 1)], min_val=0, max_val=NE - 1)
                    load_expert(o + NE, e)
            for t in range(TILES):
                sp.wait_ge(hn_done, 2 * 5 + t + 1)
                sp.dma_start(out[0, t * P:(t + 1) * P, :], hn[:, t, :]).then_inc(out_done, 16)
            sp.wait_ge(out_done, 16 * TILES)

        @block.gpsimd
        def _(pool):
            def load_gain(k):
                if k >= 2:
                    pool.wait_ge(hn_done, 2 * (k - 2) + 2)
                pool.dma_start(gain[:, k % 2, :], bass.AP(gains[k].tensor, gains[k].offset, [[0, P], [1, D]]))\
                    .then_inc(gain_in[k % 2], 16)

            load_gain(0)
            load_gain(1)
            pool.dma_start(sm[:, 496:508], bass.AP(swa_sinks.tensor, swa_sinks.offset, [[0, P], [1, NH]]))\
                .then_inc(sink_in, 16)
            pool.wait_ge(rows_sb, 4)
            pool.dma_start(bias_rows[0], rows[0:NH, 0, :]).then_inc(rows_out, 16)
            for g in range(3):
                pool.dma_start(bias_rows[1][4 * g:4 * g + 4, :], rows[0:4, 1 + g, :]).then_inc(rows_out, 16)
            pool.wait_ge(rows_out, 64)

            def load_bias(layer):
                b = bias_rows[layer]
                for n in range(3):
                    src = bass.AP(b.tensor, b.offset + 4 * n * RLEN, [[1, P], [RLEN, 4], [1, SEQ]])
                    pool.dma_start(bias[:, 4 * n:4 * n + 4, :], src).then_inc(bias_in, 16)

            load_bias(0)
            load_gain(2)
            load_gain(3)
            pool.wait_ge(s_done, ITEMS)
            load_bias(1)
            load_gain(4)
            pool.wait_ge(cat_done, 4)
            pool.dma_start(rw[:, :, :], router[0].rearrange("(k p) e -> p k e", p=P)).then_inc(rw_in, 16)
            load_gain(5)

        @block.scalar
        def _(act):
            act.dma_start(mats[:, :], index_mats).then_inc(const_in, 16)
            act.dma_start(onehot[:, :, :], bias_onehot).then_inc(onehot_in, 16)
            act.dma_start(table[0:32, :], rel_bias_table).then_inc(table_in, 16)

            nxt = [0]
            preloads = [0]

            def cut(c, rounds):
                act.wait_ge(raw_full[c % RAW], 16 * uses(c, rounds))
                wait(act, units_done, c + RAW * rounds - CUT + 1)
                act.activation(whi[:, c % CUT, 0:span(c)], raw[:, c % RAW, 0:span(c)], ACT.Copy).then_inc(hi_ready, 1)

            def cut_upto(n):
                while nxt[0] < n:
                    cut(nxt[0], 0)
                    nxt[0] += 1

            def preload(func):
                column = 48 + preloads[0]
                preloads[0] += 1
                act.activation(stats[:, column:column + 1], eps, func)

            def norm_root(k, t, src):
                wait(act, sq_done, 2 * k + t)
                act.activation(squares[:, :], src[:, t, :], ACT.Square,
                               accum_out=ssq[:, 2 * k + t:2 * k + t + 1]).then_inc(sq_done, 1)
                act.wait_ge(sq_done, 2 * k + t + 1)
                act.activation(std[:, 2 * k + t:2 * k + t + 1], ssq[:, 2 * k + t:2 * k + t + 1], ACT.Sqrt, bias=eps,
                               scale=1.0 / D).then_inc(std_done, 1)

            def xT_hi(op, t):
                wait(act, units_done, XT_FREE[op])
                for b, half in token_banks(op, t):
                    act.wait_ge(tr_done, TR0[op] + b + 1)
                    act.activation(part(xhi, half, t), four(b), ACT.Copy).then_inc(xhi_ready, 1)

            def chunk_out(c, dst):
                cut_upto(FIRST[c] + CHUNKS[c][2] // 4 + 2)
                act.wait_ge(chunk_done, c + 1)
                act.activation(dst, ps[:, 4 + 2 * (c % 2), 0:CHUNKS[c][1]], ACT.Copy).then_inc(ev_act, 1)

            def attention(layer):
                base = ITEMS * layer
                for n in range(ITEMS + 1):
                    if n < ITEMS:
                        act.wait_ge(qkT_done, base + n + 1)
                        wait(act, s_done, base + n - 1)
                        act.activation(qk[:, n % 2, :], ps[0:HD, 0, :], ACT.Copy).then_inc(qk_ready, 1)
                    if n >= 1:
                        i = n - 1
                        bank = 3 + (base + i) % 3
                        act.wait_ge(nm_ready, base + i + 1)
                        wait(act, pT_done, base + i - 1)
                        w0 = P if i < NH else SEQ
                        for qb, (a, b) in enumerate([(0, w0), (w0, w0 + SEQ)]):
                            act.activation(probs[:, i % 2, a:b], ps[:, bank, a:b], ACT.Exp,
                                           bias=sm[:, 32 + 16 * qb + i:33 + 16 * qb + i], scale=0.125,
                                           accum_out=sm[:, 64 + 16 * qb + i:65 + 16 * qb + i]).then_inc(p_ready, 1)
                act.wait_ge(fexp_in, layer + 1)
                n = 2 * TILES * NH if layer == 0 else TILES * NH
                act.activation(sm[:, 128:128 + n], sm[:, 128:128 + n], ACT.Exp).then_inc(fexp_out, 1)

            def glu_silu(t, ev, signal, value):
                act.wait_ge(signal, value)
                act.activation(silu[:, t, :], ps[:, B_G[t], :], ACT.Silu).then_inc(silu_ready, 1)

            def glu_thi(t, ev, unit):
                act.wait_ge(t_done, ev + 1)
                wait(act, units_done, unit)
                act.activation(thi[:, :, t * P:(t + 1) * P], ps[:, B_G[t], :].rearrange("p (k t) -> p k t", k=FT),
                               ACT.Copy).then_inc(thi_ready, 1)

            act.wait_ge(const_in, 16)
            preload(ACT.Sqrt)
            act.wait_ge(mem_in, 16)
            for t in range(TILES):
                norm_root(0, t, hn)
                if t == 0:
                    cut_upto(1)
                xT_hi(T_MEM, t)
            cut_upto(2)
            act.wait_ge(x_in, 16)
            for t in range(TILES):
                norm_root(1, t, h)
            chunk_out(0, memkv[:, 0, 0, :])
            act.wait_ge(rows_mm, 1)
            for g in range(4):
                n = NH if g == 0 else 4
                act.activation(rows[0:n, g, :], ps[0:n, g, 0:RLEN], ACT.Copy, scale=8.0).then_inc(rows_sb, 1)
            chunk_out(1, memkv[:, 1, 0, :])
            for t in range(TILES):
                xT_hi(T_MIX0, t)
            preload(ACT.Exp)
            act.wait_ge(rows_out, 64)
            for c in range(C_SI, C_SO):
                chunk_out(c, proj[:, 0, CHUNKS[c][3]:CHUNKS[c][3] + CHUNKS[c][1]])
            attention(0)
            for t in range(TILES):
                xT_hi(T_CAT0, t)
            preload(ACT.Sqrt)
            cut_upto(FIRST[C_SO] + 6)
            for t in range(TILES):
                act.wait_ge(ev_dve, DVE_EV[C_SO + 1] - 1 + t)
                norm_root(2, t, h)
                xT_hi(T_FFN0, t)
            preload(ACT.Silu)
            for i in range(4):
                cut(FFN0 + 2 + i, 0)
            glu_silu(0, 0, g_done, 1)
            glu_silu(1, 1, units_done, FFN0 + 4)
            for t in range(TILES):
                glu_thi(t, t, FFN0 + 4)
            with act.Fori(1, STEPS) as s:
                for i in range(4):
                    cut(FFN0 + i, s)
                glu_silu(0, s * TILES, g_done, s + 1)
                glu_silu(1, s * TILES + 1, units_done, s * 6 + FFN0 + 2)
                for i in range(2):
                    cut(FFN0 + 4 + i, s)
                for t in range(TILES):
                    glu_thi(t, s * TILES + t, FFN0 + 4 + 6 * s)
            nxt[0] = FFN0 + FFN_UNITS
            preload(ACT.Sqrt)
            cut_upto(FIRST[C_DI] + 2)
            for t in range(TILES):
                act.wait_ge(ffn_added, 2 * t + 2)
                norm_root(3, t, h)
                xT_hi(T_MIX1, t)
            preload(ACT.Exp)
            for c in range(C_DI, C_DO):
                chunk_out(c, proj[:, 0, CHUNKS[c][3]:CHUNKS[c][3] + CHUNKS[c][1]])
            attention(1)
            for t in range(TILES):
                xT_hi(T_CAT1, t)
            preload(ACT.Sqrt)
            cut_upto(MOE0 + 2)
            for t in range(TILES):
                act.wait_ge(ev_dve, DVE_EV[-1] - 1 + t)
                norm_root(4, t, h)
                for b, half in token_banks(T_ROUTE, t):
                    act.wait_ge(tr_done, TR0[T_ROUTE] + b + 1)
                    act.activation(part(xtf, half, t), four(b), ACT.Copy).then_inc(xtf_ready, 1)
            for t in range(TILES):
                act.wait_ge(hn_done, 9 + t)
                act.activation(nhi[:, t, :], hn[:, t, :], ACT.Copy).then_inc(nhi_ready, 1)
            preload(ACT.Exp)
            cut_upto(MOE0 + 3)
            act.wait_ge(top_in, 1)
            act.activation(rt[:, 160:176], rt[:, 160:176], ACT.Exp).then_inc(top_exp, 1)
            preload(ACT.Silu)

            def gather_out(q):
                for b in range(2):
                    act.wait_ge(gx_done, 2 * q + b + 1)
                    act.activation(xhi[:, 4 * b:4 * b + 4, 0:P], four(B_X[b]), ACT.Copy).then_inc(gxhi, 1)
                act.wait_ge(put_done, q + 1)
                act.activation(put_next[:, :], ps[:, B_PUT, 0:SEQ], ACT.Copy).then_inc(put_out, 1)
                act.activation(gate_next[:, :], ps[:, B_PUT, SEQ:SEQ + 1], ACT.Copy).then_inc(put_out, 1)

            def y_hi(prev):
                act.wait_ge(units_done, prev * FFN_UNITS + FFN_UNITS + MOE0)
                for b in range(2):
                    act.activation(yhi[:, b * 512:(b + 1) * 512], ps[:, B_Y[0][b], :], ACT.Copy, scale=gate[:, 0:1])\
                        .then_inc(yhi_ready, 1)

            def expert(prev=None):
                first = prev is None
                job = 0 if first else prev + 1
                r = job * STEPS
                if first:
                    for i in range(3, 6):
                        cut(MOE0 + i, 0)
                else:
                    for i in range(2):
                        cut(MOE0 + i, r)
                    y_hi(prev)
                    for i in range(2, 6):
                        cut(MOE0 + i, r)
                glu_silu(0, r + EV_MOE, units_done, r * 6 + MOE0 + 4)
                if not first:
                    act.wait_ge(sc_done, 4 * prev + 4)
                act.wait_ge(put_out, 2 * job + 2)
                act.activation(put[:, :], put_next[:, :], ACT.Copy).then_inc(put_now, 1)
                act.activation(gate[:, :], gate_next[:, :], ACT.Copy).then_inc(put_now, 1)
                glu_thi(0, r + EV_MOE, r * 6 + MOE0 + 4)
                with act.Fori(1, STEPS) as s:
                    rs = s + job * STEPS
                    for i in range(4):
                        cut(MOE0 + i, rs)
                    glu_silu(0, rs + EV_MOE, units_done, rs * 6 + MOE0 + 2)
                    for i in range(2):
                        cut(MOE0 + 4 + i, rs)
                    glu_thi(0, rs + EV_MOE, rs * 6 + MOE0 + 4)
                gather_out(job + 1)

            gather_out(0)
            expert()
            act.wait_ge(table_ready, 1)
            more = act.value_load(jobs_i[0:1, 0:1], min_val=NE - 1, max_val=JOBS - 1)
            with act.Fori(0, more) as prev:
                expert(prev)
            preload(ACT.Sqrt)
            y_hi(more)
            for t in range(TILES):
                act.wait_ge(h_added, 4 * more + 2 + 2 * t)
                norm_root(5, t, h)

        @block.vector
        def _(dve):
            nxt = [0]
            chain = [0]

            def link(ins):
                chain[0] += 1
                ins.then_inc(dve_chain, 1)
                dve.wait_ge(dve_chain, chain[0])

            def cut(c, rounds):
                dve.wait_ge(hi_ready, c + RAW * rounds + 1)
                n = span(c)
                dve.tensor_tensor(wlo[:, c % CUT, 0:n], raw[:, c % RAW, 0:n], whi[:, c % CUT, 0:n].bitcast(F32),
                                  ALU.subtract).then_inc(lo_ready, 1)

            def cut_upto(n):
                while nxt[0] < n:
                    cut(nxt[0], 0)
                    nxt[0] += 1

            def norm(k, t, src):
                dve.wait_ge(std_done, 2 * k + t + 1)
                dve.reciprocal(rstd[:, 2 * k + t:2 * k + t + 1], std[:, 2 * k + t:2 * k + t + 1]).then_inc(rstd_done, 1)
                dve.wait_ge(rstd_done, 2 * k + t + 1)
                dve.wait_ge(gain_in[k % 2], 16 * (k // 2 + 1))
                dve.scalar_tensor_tensor(hn[:, t, :], src[:, t, :], rstd[:, 2 * k + t:2 * k + t + 1],
                                         gain[:, k % 2, :], ALU.mult, ALU.mult).then_inc(hn_done, 1)

            def xT_lo(op, t):
                for b, half in token_banks(op, t):
                    dve.wait_ge(xhi_ready, TR0[op] + b + 1)
                    dve.tensor_tensor(part(xlo, half, t), four(b), part(xhi, half, t).bitcast(F32), ALU.subtract)\
                        .then_inc(xlo_ready, 1)

            def chunk_out(c, dst):
                cut_upto(FIRST[c] + CHUNKS[c][2] // 4 + 2)
                dve.wait_ge(units_done, FIRST[c] + CHUNKS[c][2] // 4)
                dve.tensor_copy(dst, ps[:, 5 + 2 * (c % 2), 0:CHUNKS[c][1]]).then_inc(ev_dve, 1)

            def chunk_add(c, t):
                cols = slice(CHUNKS[c][3], CHUNKS[c][3] + 512)
                if t == 0:
                    dve.wait_ge(chunk_done, c + 1)
                else:
                    dve.wait_ge(units_done, FIRST[c] + CHUNKS[c][2] // 4)
                dve.tensor_tensor(h[:, t, cols], h[:, t, cols], ps[:, 4 + 2 * (c % 2) + t, :], ALU.add)\
                    .then_inc(ev_dve, 1)

            nm = sm[:, 32:64].rearrange("p (q i) -> p q i", q=2)
            den = sm[:, 64:96].rearrange("p (q i) -> p q i", q=2)
            wts = sm[:, 96:128].rearrange("p (q i) -> p q i", q=2)

            def attention(layer):
                base = ITEMS * layer
                for n in range(1, ITEMS + 3):
                    i = n - 1
                    if i < ITEMS:
                        dve.wait_ge(s_done, base + i + 1)
                        bank = 3 + (base + i) % 3
                        w0 = P if i < NH else SEQ
                        for qb, (a, b) in enumerate([(0, w0), (w0, w0 + SEQ)]):
                            dve.tensor_reduce(sm[:, 16 * qb + i:16 * qb + i + 1], ps[:, bank, a:b], AX.X, ALU.max,
                                              negate=True).then_inc(nmr_done, 1)
                        dve.wait_ge(nmr_done, 2 * (base + i + 1))
                        dve.tensor_scalar(free(sm[:, 32 + i:33 + i], (16, 2)), free(sm[:, i:i + 1], (16, 2)), 0.125,
                                          None, ALU.mult).then_inc(nm_ready, 1)
                    i = n - 2
                    if 0 <= i < ITEMS:
                        dve.wait_ge(pT_done, base + i + 1)
                        wait(dve, o_done, base + i - 1)
                        w = 384 if i < NH else 512
                        dve.tensor_copy(probsT[:, i % 2, 0:w], ps[:, 1 + (base + i) % 2, 0:w]).then_inc(pT_ready, 1)
                    if n in (6, 10, 14):
                        heads_out(layer, (n - 6) // 4)
                heads_out(layer, 3)

            def heads_out(layer, g):
                n = 4 * layer + g
                dve.wait_ge(o_done, 4 * (n + 1))
                dve.tensor_copy(oraw[:, :, 4 * g:4 * g + 4, :].rearrange("p q i d -> p q (i d)"),
                                ps[:, 6 + n % 2, :].rearrange("p (q c) -> p q c", q=2)).then_inc(o_out, 1)

            def combine0():
                f = sm[:, 128:152].rearrange("p (q i) -> p q i", q=2)
                es = sm[:, 152:176].rearrange("p (q i) -> p q i", q=2)
                nm2 = sm[:, 176:200].rearrange("p (q i) -> p q i", q=2)
                tmp = sm[:, 200:224].rearrange("p (q i) -> p q i", q=2)
                sink2 = free(sm[:, 256:257], (0, 2), (1, NH))
                dve.wait_ge(sink_in, 16)
                link(dve.tensor_scalar(sm[:, 256:268], sm[:, 496:508], -1.0, None, ALU.mult))
                link(dve.tensor_tensor(nm2, nm[:, :, 0:NH], sink2, ALU.min))
                dve.tensor_tensor(f, nm2, nm[:, :, 0:NH], ALU.subtract)
                dve.tensor_tensor(es, nm2, sink2, ALU.subtract).then_inc(fexp_in, 1)
                dve.wait_ge(fexp_out, 1)
                link(dve.tensor_tensor(tmp, f, den[:, :, 0:NH], ALU.mult))
                link(dve.tensor_tensor(tmp, tmp, es, ALU.add))
                link(dve.reciprocal(tmp, tmp))
                dve.tensor_tensor(wts[:, :, 0:NH], f, tmp, ALU.mult)
                link(dve.reciprocal(wts[:, :, NH:], den[:, :, NH:]))
                for t in range(TILES):
                    dve.tensor_tensor(hn[:, t, :].rearrange("p (i d) -> p i d", i=ITEMS), oraw[:, t, :, :],
                                      free(sm[:, 96 + 16 * t:97 + 16 * t], (1, ITEMS), (0, HD)), ALU.mult)\
                        .then_inc(cat_done, 1)

            def combine1():
                f = sm[:, 128:152].rearrange("p (q g i) -> p q g i", q=2, g=3)
                low = sm[:, 176:184].rearrange("p (q i) -> p q i", q=2)
                tmp = sm[:, 200:224].rearrange("p (q g i) -> p q g i", q=2, g=3)
                tot = sm[:, 184:192].rearrange("p (q i) -> p q i", q=2)
                link(dve.tensor_tensor(low, nm[:, :, 0:4], nm[:, :, 4:8], ALU.min))
                link(dve.tensor_tensor(low, low, nm[:, :, 8:12], ALU.min))
                for g in range(3):
                    last = dve.tensor_tensor(f[:, :, g, :], low, nm[:, :, 4 * g:4 * g + 4], ALU.subtract)
                last.then_inc(fexp_in, 1)
                dve.wait_ge(fexp_out, 2)
                link(dve.tensor_tensor(sm[:, 200:224].rearrange("p (q i) -> p q i", q=2),
                                       sm[:, 128:152].rearrange("p (q i) -> p q i", q=2), den[:, :, 0:NH], ALU.mult))
                link(dve.tensor_tensor(tot, tmp[:, :, 0, :], tmp[:, :, 1, :], ALU.add))
                link(dve.tensor_tensor(tot, tot, tmp[:, :, 2, :], ALU.add))
                link(dve.reciprocal(tot, tot))
                for g in range(3):
                    dve.tensor_tensor(wts[:, :, 4 * g:4 * g + 4], f[:, :, g, :], tot, ALU.mult)
                link(dve.reciprocal(wts[:, :, NH:], den[:, :, NH:]))
                half = NH * HD
                for t in range(TILES):
                    link(dve.tensor_tensor(oraw[:, t, 0:NH, :], oraw[:, t, 0:NH, :],
                                           free(sm[:, 96 + 16 * t:97 + 16 * t], (1, NH), (0, HD)), ALU.mult))
                    o = oraw[:, t, :, :].rearrange("p i d -> p (i d)")
                    link(dve.tensor_tensor(hn[:, t, 0:256], o[:, 0:256], o[:, 256:512], ALU.add))
                    dve.tensor_tensor(hn[:, t, 0:256], hn[:, t, 0:256], o[:, 512:half], ALU.add)
                    dve.tensor_tensor(hn[:, t, 256:512].rearrange("p (i d) -> p i d", i=MH), oraw[:, t, NH:, :],
                                      free(sm[:, 108 + 16 * t:109 + 16 * t], (1, MH), (0, HD)), ALU.mult)\
                        .then_inc(cat_done, 1)

            def glu_mul(t, ev):
                dve.wait_ge(silu_ready, ev + 1)
                dve.tensor_tensor(act_h[:, t, :], ps[:, B_U[t], :], silu[:, t, :], ALU.mult).then_inc(act_ready, 1)

            def glu_tlo(t, ev):
                dve.wait_ge(thi_ready, ev + 1)
                dve.tensor_tensor(tlo[:, :, t * P:(t + 1) * P], ps[:, B_G[t], :].rearrange("p (k t) -> p k t", k=FT),
                                  thi[:, :, t * P:(t + 1) * P].bitcast(F32), ALU.subtract).then_inc(tlo_ready, 1)

            dve.memset(table[32:33, :], 1.0).then_inc(table_one, 1)
            for t in range(TILES):
                norm(0, t, hn)
                if t == 0:
                    cut_upto(1)
                xT_lo(T_MEM, t)
            cut_upto(2)
            for t in range(TILES):
                norm(1, t, h)
            chunk_out(0, memkv[:, 0, 1, :])
            chunk_out(1, memkv[:, 1, 1, :])
            for t in range(TILES):
                xT_lo(T_MIX0, t)
            dve.wait_ge(rows_out, 64)
            for c in range(C_SI, C_SO):
                chunk_out(c, proj[:, 1, CHUNKS[c][3]:CHUNKS[c][3] + CHUNKS[c][1]])
            attention(0)
            combine0()
            for t in range(TILES):
                xT_lo(T_CAT0, t)
            cut_upto(FIRST[C_SO + 1] + 2)
            for t in range(TILES):
                chunk_add(C_SO, t)
            cut_upto(FFN0 + 2)
            chunk_add(C_SO + 1, 0)
            norm(2, 0, h)
            chunk_add(C_SO + 1, 1)
            xT_lo(T_FFN0, 0)
            norm(2, 1, h)
            xT_lo(T_FFN0, 1)
            dve.memset(zero[:, :].bitcast(F32), 0.0).then_inc(zero_set, 1)
            for i in range(4):
                cut(FFN0 + 2 + i, 0)
            for t in range(TILES):
                glu_mul(t, t)
            for t in range(TILES):
                glu_tlo(t, t)
            with dve.Fori(1, STEPS) as s:
                for i in range(4):
                    cut(FFN0 + i, s)
                for t in range(TILES):
                    glu_mul(t, s * TILES + t)
                for i in range(2):
                    cut(FFN0 + 4 + i, s)
                for t in range(TILES):
                    glu_tlo(t, s * TILES + t)
            nxt[0] = FFN0 + FFN_UNITS
            cut_upto(FIRST[C_DI] + 2)

            def ffn_add(t):
                if t == 0:
                    dve.wait_ge(y0_done, 1)
                else:
                    dve.wait_ge(units_done, FFN0 + FFN_UNITS)
                for b in range(2):
                    dve.tensor_tensor(h[:, t, b * 512:(b + 1) * 512], h[:, t, b * 512:(b + 1) * 512],
                                      ps[:, B_Y[t][b], :], ALU.add).then_inc(ffn_added, 1)

            ffn_add(0)
            norm(3, 0, h)
            ffn_add(1)
            xT_lo(T_MIX1, 0)
            norm(3, 1, h)
            xT_lo(T_MIX1, 1)
            for c in range(C_DI, C_DO):
                chunk_out(c, proj[:, 1, CHUNKS[c][3]:CHUNKS[c][3] + CHUNKS[c][1]])
            attention(1)
            combine1()
            for t in range(TILES):
                xT_lo(T_CAT1, t)
            cut_upto(MOE0)
            for t in range(TILES):
                chunk_add(C_DO, t)
            cut_upto(MOE0 + 1)
            chunk_add(C_DO + 1, 0)
            norm(4, 0, h)
            chunk_add(C_DO + 1, 1)
            cut_upto(MOE0 + 2)
            norm(4, 1, h)

            dve.memset(zero[:, :].bitcast(F32), 0.0).then_inc(zero_set, 1)
            dve.memset(pos[:, :, :], -1.0)
            link(dve.memset(comb[:, :, :], 0.0))

            def n_lo(t):
                dve.wait_ge(nhi_ready, t + 1)
                dve.tensor_tensor(nlo[:, t, :], hn[:, t, :], nhi[:, t, :].bitcast(F32), ALU.subtract)\
                    .then_inc(nlo_ready, 1)

            l3 = rt[:, 0:16].rearrange("p (t e) -> p t e", t=2)
            gt, eq = rt[:, 32:160], rt[:, 192:320]
            ex = rt[:, 160:176].rearrange("p (t e) -> p t e", t=2)
            rank, sel = rt[:, 320:336], rt[:, 336:352]
            top, tot = rt[:, 352:354], rt[:, 354:356]
            tri3 = tri.rearrange("p (e f) -> p e f", e=NE)
            n_lo(0)
            dve.wait_ge(logit_done, 1)
            link(dve.tensor_copy(l3, free(ps[:, B_LG[0], 0:1], (512 * (B_LG[1] - B_LG[0]), 2), (1, NE))))
            other = free(rt[:, 0:1], (NE, 2), (0, NE), (1, NE))
            own = free(rt[:, 0:1], (NE, 2), (1, NE), (0, NE))
            cube = [free(a[:, 0:1], (64, 2), (NE, NE), (1, NE)) for a in (gt, eq)]
            dve.tensor_tensor(cube[0], other, own, ALU.is_gt)
            link(dve.tensor_tensor(cube[1], other, own, ALU.is_equal))
            link(dve.tensor_tensor(eq.rearrange("p (t c) -> p t c", t=2), eq.rearrange("p (t c) -> p t c", t=2),
                                   free(tri[:, 0:1], (0, 2), (1, 64)), ALU.mult))
            link(dve.tensor_tensor(gt, gt, eq, ALU.add))
            dve.tensor_reduce(top, l3, AX.X, ALU.max)
            link(dve.tensor_reduce(rank, gt.rearrange("p (t f) -> p t f", f=NE), AX.X, ALU.add))
            dve.tensor_scalar(sel, rank, 2.0, None, ALU.is_lt).then_inc(rank_in, 1)
            dve.tensor_tensor(ex, l3, free(top, (1, 2), (0, NE)), ALU.subtract).then_inc(top_in, 1)
            n_lo(1)
            dve.wait_ge(rank_in, 1)
            dve.wait_ge(rank_done, 1)
            p1 = rt[:, 368:384].rearrange("p (t e) -> p t e", t=2)
            over = rt[:, 384:392]
            link(dve.scalar_tensor_tensor(rt[:, 368:384], ps[:, B_RANK, 0:16], 1.0, sel, ALU.add, ALU.mult))
            link(dve.tensor_scalar(pos[:, :, 0:NE], p1, -1.0, None, ALU.add))
            for t in range(TILES):
                dve.tensor_scalar(pick[:, t, :], iota, pos[:, t, 0:1], None, ALU.is_equal).then_inc(pick_ready, 1)

            def combine_gates():
                dve.wait_ge(top_exp, 1)
                link(dve.tensor_tensor(ex, ex, sel.rearrange("p (t e) -> p t e", t=2), ALU.mult))
                link(dve.tensor_reduce(tot, ex, AX.X, ALU.add))
                link(dve.reciprocal(tot, tot))
                link(dve.tensor_tensor(comb[:, :, 0:NE], ex, free(tot, (1, 2), (0, NE)), ALU.mult))
                dve.tensor_scalar(over, ps[:, B_RANK, 16:24], float(P), None, ALU.is_gt).then_inc(comb_ready, 1)

            def table_of_jobs():
                dve.wait_ge(comb_ready, 1)
                om = rt[:, 400:464].rearrange("p (e f) -> p e f", e=NE)
                link(dve.tensor_tensor(om, free(over, (0, NE), (1, NE)), tri3, ALU.mult))
                link(dve.tensor_reduce(rt[:, 392:400], om, AX.X, ALU.add))
                oh = rt[:, 464:464 + NE * MAX_OVER]
                for o in range(MAX_OVER):
                    last = dve.scalar_tensor_tensor(oh[:, NE * o:NE * o + NE], rt[:, 392:400], float(o), over,
                                                    ALU.is_equal, ALU.mult)
                link(last)
                oh3 = oh.rearrange("p (o e) -> p o e", e=NE)
                pr = rt[:, 512:512 + NE * MAX_OVER].rearrange("p (o e) -> p o e", e=NE)
                red = rt[:, 560:560 + MAX_OVER]
                for t in range(TILES):
                    link(dve.tensor_tensor(pr, oh3, free(rt[:, 368 + 8 * t:369 + 8 * t], (0, MAX_OVER), (1, NE)),
                                           ALU.mult))
                    link(dve.tensor_reduce(red, pr, AX.X, ALU.add))
                    link(dve.tensor_scalar(pos[:, t, NE:JOBS], red, -1.0 - P, None, ALU.add))
                    link(dve.tensor_tensor(pr, oh3, free(comb[:, t, 0:1], (0, MAX_OVER), (1, NE)), ALU.mult))
                    link(dve.tensor_reduce(comb[:, t, NE:JOBS], pr, AX.X, ALU.add))
                link(dve.tensor_tensor(pr, oh3, free(expert_no, (0, MAX_OVER), (1, NE)), ALU.mult))
                dve.tensor_reduce(rt[:, 570:570 + MAX_OVER], pr, AX.X, ALU.add)
                link(dve.tensor_reduce(rt[:, 569:570], over, AX.X, ALU.add))
                link(dve.tensor_scalar(rt[:, 568:569], rt[:, 569:570], NE - 1.0, None, ALU.add))
                dve.tensor_copy(jobs_i[0:1, 0:2 + MAX_OVER], rt[0:1, 568:570 + MAX_OVER]).then_inc(table_ready, 1)

            def build_pick(q):
                wait(dve, put_done, q)
                for t in range(TILES):
                    dve.tensor_scalar(pick[:, t, :], iota, pos[:, t, bass.ds(q, 1)], None, ALU.is_equal)\
                        .then_inc(pick_ready, 1)

            def gather_lo(q):
                for b in range(2):
                    dve.wait_ge(gxhi, 2 * q + b + 1)
                    dve.tensor_tensor(xlo[:, 4 * b:4 * b + 4, 0:P], four(B_X[b]),
                                      xhi[:, 4 * b:4 * b + 4, 0:P].bitcast(F32), ALU.subtract).then_inc(gxlo, 1)

            def y_lo(prev):
                for b in range(2):
                    dve.wait_ge(yhi_ready, 2 * prev + 1 + b)
                    dve.scalar_tensor_tensor(ylo[:, b * 512:(b + 1) * 512], ps[:, B_Y[0][b], :], gate[:, 0:1],
                                             yhi[:, b * 512:(b + 1) * 512].bitcast(F32), ALU.mult, ALU.subtract)\
                        .then_inc(ylo_ready, 1)

            def add_scattered(prev):
                for n in range(4):
                    dve.wait_ge(sc_done, 4 * prev + 1 + n)
                    t, b = n // 2, n % 2
                    dve.tensor_tensor(h[:, t, b * 512:(b + 1) * 512], h[:, t, b * 512:(b + 1) * 512],
                                      ps[:, B_SC[n], :], ALU.add).then_inc(h_added, 1)

            def expert(prev=None):
                first = prev is None
                job = 0 if first else prev + 1
                r = job * STEPS
                if first:
                    table_of_jobs()
                    build_pick(1)
                    for i in range(3, 6):
                        cut(MOE0 + i, 0)
                    glu_mul(0, EV_MOE)
                else:
                    for i in range(2):
                        cut(MOE0 + i, r)
                    y_lo(prev)
                    build_pick(job + 1)
                    for i in range(2, 6):
                        cut(MOE0 + i, r)
                    glu_mul(0, r + EV_MOE)
                    add_scattered(prev)
                glu_tlo(0, r + EV_MOE)
                with dve.Fori(1, STEPS) as s:
                    rs = s + job * STEPS
                    for i in range(4):
                        cut(MOE0 + i, rs)
                    glu_mul(0, rs + EV_MOE)
                    for i in range(2):
                        cut(MOE0 + 4 + i, rs)
                    glu_tlo(0, rs + EV_MOE)
                gather_lo(job + 1)

            cut_upto(MOE0 + 3)
            combine_gates()
            gather_lo(0)
            expert()
            dve.wait_ge(table_ready, 1)
            more = dve.value_load(jobs_i[0:1, 0:1], min_val=NE - 1, max_val=JOBS - 1)
            with dve.Fori(0, more) as prev:
                expert(prev)
            y_lo(more)
            add_scattered(more)
            for t in range(TILES):
                norm(5, t, h)

        @block.tensor
        def _(pe):
            def three(dst, ahi, alo, bhi, blo, start, stop):
                pe.matmul(dst, ahi, bhi, start=start, stop=False)
                pe.matmul(dst, ahi, blo, start=False, stop=False)
                return pe.matmul(dst, alo, bhi, start=False, stop=stop)

            def transpose_x(op, t):
                for b, half in token_banks(op, t):
                    for j in range(4):
                        kt = 4 * half + j
                        last = pe.transpose(ps[:, b, j * P:(j + 1) * P], hn[:, t, kt * P:(kt + 1) * P], ident)
                    last.then_inc(tr_done, 1)

            def norm_transposed(k, op, t):
                pe.wait_ge(hn_done, 2 * k + t + 1)
                transpose_x(op, t)

            def chunk(c, op=None, between=None):
                _, width, rows_, _ = CHUNKS[c]
                if c >= 2:
                    pe.wait_ge(ev_act, ACT_EV[c - 2])
                    pe.wait_ge(ev_dve, DVE_EV[c - 2])
                n_units = rows_ // 4
                if op is None:
                    order = [(i, t) for i in range(n_units) for t in range(TILES)]
                else:
                    order = [(i, t) for t in range(TILES) for i in range(n_units)]
                for step, (i, t) in enumerate(order):
                    u = FIRST[c] + i
                    pe.wait_ge(lo_ready, u + 1)
                    if op is not None:
                        pe.wait_ge(xlo_ready, TR0[op] + t * n_units + i + 1)
                    dst = ps[:, 4 + 2 * (c % 2) + t, 0:width]
                    for j in range(4):
                        kt = 4 * i + j
                        cols = slice(j * width, (j + 1) * width)
                        last = three(dst, xhi[:, kt, t * P:(t + 1) * P], xlo[:, kt, t * P:(t + 1) * P],
                                     whi[:, u % CUT, cols], wlo[:, u % CUT, cols], kt == 0, kt == 4 * n_units - 1)
                    if t == TILES - 1:
                        last.then_inc(units_done, 1)
                    elif i == n_units - 1:
                        last.then_inc(chunk_done, 1)
                    if step == 0 and between is not None:
                        between()

            def attention(layer):
                base = ITEMS * layer
                for n in range(ITEMS + 3):
                    if n < ITEMS:
                        q, k, _ = items[layer][n]
                        wait(pe, qk_ready, base + n)
                        for t in range(TILES):
                            pe.transpose(ps[0:HD, 0, t * P:(t + 1) * P], proj[:, t, q:q + HD], ident)
                        for t in range(TILES):
                            last = pe.transpose(ps[0:HD, 0, SEQ + t * P:SEQ + (t + 1) * P], kv(layer, n, t, k), ident)
                        last.then_inc(qkT_done, 1)
                    i = n - 1
                    if 0 <= i < ITEMS:
                        pe.wait_ge(qk_ready, base + i + 1)
                        wait(pe, p_ready, 2 * (base + i - 2))
                        if i == 0:
                            pe.wait_ge(bias_in, 48 * (layer + 1))
                        bank = 3 + (base + i) % 3
                        w0 = P if i < NH else SEQ
                        for qb in range(TILES):
                            nk = w0 if qb == 0 else SEQ
                            dst = ps[:, bank, qb * w0:qb * w0 + nk]
                            last = pe.matmul(dst, qk[:, i % 2, qb * P:(qb + 1) * P], qk[:, i % 2, SEQ:SEQ + nk],
                                             start=True, stop=i >= NH)
                            if i < NH:
                                last = pe.matmul(dst, anti, bias[:, i, SEQ - nk:SEQ], start=False, stop=True)
                        last.then_inc(s_done, 1)
                    i = n - 2
                    if 0 <= i < ITEMS:
                        pe.wait_ge(p_ready, 2 * (base + i + 1))
                        wait(pe, pT_ready, base + i - 1)
                        for j in range(3 if i < NH else 4):
                            last = pe.transpose(ps[:, 1 + (base + i) % 2, j * P:(j + 1) * P],
                                                probs[:, i % 2, j * P:(j + 1) * P], ident)
                        last.then_inc(pT_done, 1)
                    i = n - 3
                    if 0 <= i < ITEMS:
                        pe.wait_ge(pT_ready, base + i + 1)
                        wait(pe, o_out, (base + i) // 4 - 1)
                        v = items[layer][i][2]
                        blocks = [[0], [0, 1]] if i < NH else [[0, 1], [0, 1]]
                        j = 0
                        for qb in range(TILES):
                            for m in blocks[qb]:
                                c0 = qb * SEQ + i % 4 * HD
                                last = pe.matmul(ps[:, 6 + (base + i) // 4 % 2, c0:c0 + HD],
                                                 probsT[:, i % 2, j * P:(j + 1) * P], kv(layer, i, m, v),
                                                 start=m == 0, stop=m == blocks[qb][-1])
                                j += 1
                        last.then_inc(o_done, 1)

            def in_tile(c, rounds, t, bank, half):
                for j in range(4):
                    kt = 4 * half + j
                    cols = slice(j * FCH, (j + 1) * FCH)
                    last = three(ps[:, bank[t], :], xhi[:, kt, t * P:(t + 1) * P], xlo[:, kt, t * P:(t + 1) * P],
                                 whi[:, c % CUT, cols], wlo[:, c % CUT, cols], kt == 0, kt == KT - 1)
                return last

            def unit_in(c, rounds, tiles, bank, half, first_tile_done=None):
                pe.wait_ge(lo_ready, c + RAW * rounds + 1)
                for t in range(tiles):
                    last = in_tile(c, rounds, t, bank, half)
                    if first_tile_done is not None and t == 0:
                        last.then_inc(first_tile_done, 1)
                last.then_inc(units_done, 1)

            def out_tile(c, t, half, final):
                for j in range(2):
                    ft = 2 * half + j
                    for b in range(2):
                        cols = slice(j * D + b * 512, j * D + b * 512 + 512)
                        last = three(ps[:, B_Y[t][b], :], thi[:, ft, t * P:(t + 1) * P],
                                     tlo[:, ft, t * P:(t + 1) * P], whi[:, c % CUT, cols], wlo[:, c % CUT, cols],
                                     False, final and half == 1 and j == 1)
                return last

            def unit_out(c, rounds, tiles, half, final=False):
                pe.wait_ge(lo_ready, c + RAW * rounds + 1)
                for t in range(tiles):
                    last = out_tile(c, t, half, final)
                last.then_inc(units_done, 1)

            def hidden_t(t, ev):
                pe.wait_ge(act_ready, ev + 1)
                for j in range(FT):
                    last = pe.transpose(ps[:, B_G[t], j * P:(j + 1) * P], act_h[:, t, j * P:(j + 1) * P], ident)
                last.then_inc(t_done, 1)

            def products_in(c, rounds, tiles, ev=None):
                for i in range(2):
                    unit_in(c + i, rounds, tiles, B_U, i)
                if ev is not None:
                    pe.wait_ge(tlo_ready, ev)
                unit_in(c + 2, rounds, tiles, B_G, 0)
                unit_in(c + 3, rounds, tiles, B_G, 1, g_done if tiles > 1 else None)

            def clear_y(tiles):
                for t in range(tiles):
                    for b in range(2):
                        pe.matmul(ps[:, B_Y[t][b], :], zero[:, 0:P], zero[:, :], start=True, stop=False)

            pe.wait_ge(const_in, 16)
            norm_transposed(0, T_MEM, 0)
            chunk(0, T_MEM, lambda: norm_transposed(0, T_MEM, 1))
            pe.wait_ge(onehot_in, 16)
            pe.wait_ge(table_in, 16)
            pe.wait_ge(table_one, 1)
            for g in range(4):
                n = NH if g == 0 else 4
                heads = table[:, 0:NH] if g == 0 else table[:, 4 * g - 4:4 * g]
                last = pe.matmul(ps[0:n, g, 0:RLEN], heads, onehot[:, g, :], start=True, stop=True)
            last.then_inc(rows_mm, 1)

            def x_transposed():
                pe.wait_ge(rows_sb, 4)
                for t in range(TILES):
                    norm_transposed(1, T_MIX0, t)

            chunk(1, None, x_transposed)
            pe.wait_ge(xlo_ready, TR0[T_MIX0 + 1])
            for c in range(C_SI, C_SO):
                chunk(c)
            pe.wait_ge(ev_act, ACT_EV[C_SO - 1])
            pe.wait_ge(ev_dve, DVE_EV[C_SO - 1])
            attention(0)
            def mixed_transposed(layer, op, t):
                pe.wait_ge(cat_done, 2 * layer + t + 1)
                transpose_x(op, t)

            mixed_transposed(0, T_CAT0, 0)
            chunk(C_SO, T_CAT0, lambda: mixed_transposed(0, T_CAT0, 1))
            chunk(C_SO + 1)
            norm_transposed(2, T_FFN0, 0)
            for t in range(TILES):
                for i in range(2):
                    pe.wait_ge(lo_ready, FFN0 + i + 1)
                    pe.wait_ge(xlo_ready, TR0[T_FFN0] + 2 * t + i + 1)
                    last = in_tile(FFN0 + i, 0, t, B_U, i)
                    if t == 1:
                        last.then_inc(units_done, 1)
                    elif i == 0:
                        norm_transposed(2, T_FFN0, 1)
            unit_in(FFN0 + 2, 0, TILES, B_G, 0)
            unit_in(FFN0 + 3, 0, TILES, B_G, 1, g_done)
            pe.wait_ge(zero_set, 1)
            clear_y(TILES)
            for t in range(TILES):
                hidden_t(t, t)
            with pe.Fori(1, STEPS) as s:
                products_in(FFN0 - 2, s, TILES, s * TILES)
                unit_out(FFN0 + 2, s, TILES, 0)
                for t in range(TILES):
                    hidden_t(t, s * TILES + t)
                unit_out(FFN0 + 3, s, TILES, 1)
            pe.wait_ge(tlo_ready, EV_MOE)
            for t in range(TILES):
                for i in range(2):
                    u = FFN0 + FFN_UNITS - 2 + i
                    pe.wait_ge(lo_ready, u + 1)
                    last = out_tile(u, t, i, True)
                    if t == 1:
                        last.then_inc(units_done, 1)
                    elif i == 1:
                        last.then_inc(y0_done, 1)
            norm_transposed(3, T_MIX1, 0)
            chunk(C_DI, T_MIX1, lambda: norm_transposed(3, T_MIX1, 1))
            for c in range(C_DI + 1, C_DO):
                chunk(c)
            pe.wait_ge(ev_act, ACT_EV[C_DO - 1])
            pe.wait_ge(ev_dve, DVE_EV[C_DO - 1])
            attention(1)
            mixed_transposed(1, T_CAT1, 0)
            chunk(C_DO, T_CAT1, lambda: mixed_transposed(1, T_CAT1, 1))
            chunk(C_DO + 1)
            pe.wait_ge(rw_in, 16)
            for t in range(TILES):
                norm_transposed(4, T_ROUTE, t)
                for kt in range(KT):
                    if kt % 4 == 0:
                        pe.wait_ge(xtf_ready, 2 * t + kt // 4 + 1)
                    last = pe.matmul(ps[:, B_LG[t], 0:NE], xtf[:, kt, t * P:(t + 1) * P], rw[:, kt, :],
                                     start=kt == 0, stop=kt == KT - 1)
            last.then_inc(logit_done, 1)
            pe.wait_ge(rank_in, 1)
            sel = [rt[:, 336 + NE * t:336 + NE * (t + 1)] for t in range(TILES)]
            pe.matmul(ps[:, B_RANK, 2 * NE:3 * NE], ones, sel[0], start=True, stop=False)
            pe.matmul(ps[:, B_RANK, 2 * NE:3 * NE], ones, sel[1], start=False, stop=True)
            pe.matmul(ps[:, B_RANK, 0:NE], before, sel[0], start=True, stop=True)
            pe.matmul(ps[:, B_RANK, NE:2 * NE], ones, sel[0], start=True, stop=False)
            pe.matmul(ps[:, B_RANK, NE:2 * NE], before, sel[1], start=False, stop=True).then_inc(rank_done, 1)

            def gather(q):
                pe.wait_ge(pick_ready, 2 * q + 2)
                for kt in range(KT):
                    dst = ps[:, B_X[kt // 4], kt % 4 * P:(kt % 4 + 1) * P]
                    for n, (t, part) in enumerate([(t, part) for t in range(TILES) for part in (nhi, nlo)]):
                        last = pe.matmul(dst, part[:, t, kt * P:(kt + 1) * P], pick[:, t, :], start=n == 0, stop=n == 3)
                    if kt % 4 == 3:
                        last.then_inc(gx_done, 1)
                for t in range(TILES):
                    pe.transpose(ps[:, B_PUT, t * P:(t + 1) * P], pick[:, t, :].bitcast(F32), ident)
                pe.wait_ge(comb_ready, 1)
                for t in range(TILES):
                    last = pe.matmul(ps[:, B_PUT, SEQ:SEQ + 1], pick[:, t, :].bitcast(F32), comb[:, t, bass.ds(q, 1)],
                                     start=t == 0, stop=t == 1)
                last.then_inc(put_done, 1)

            def scatter(prev):
                pe.wait_ge(put_now, 2 * prev + 2)
                pe.wait_ge(ylo_ready, 2 * prev + 2)
                pe.wait_ge(put_out, 2 * prev + 4)
                for n in range(4):
                    t, b = n // 2, n % 2
                    pe.matmul(ps[:, B_SC[n], :], put[:, t * P:(t + 1) * P], yhi[:, b * 512:(b + 1) * 512],
                              start=True, stop=False)
                    pe.matmul(ps[:, B_SC[n], :], put[:, t * P:(t + 1) * P], ylo[:, b * 512:(b + 1) * 512],
                              start=False, stop=True).then_inc(sc_done, 1)

            def expert(prev=None):
                first = prev is None
                job = 0 if first else prev + 1
                r = job * STEPS
                pe.wait_ge(gxlo, 2 * job + 2)
                products_in(MOE0, r, 1)
                if not first:
                    scatter(prev)
                clear_y(1)
                hidden_t(0, r + EV_MOE)
                with pe.Fori(1, STEPS) as s:
                    rs = s + job * STEPS
                    products_in(MOE0 - 2, rs, 1, rs + EV_MOE)
                    unit_out(MOE0 + 2, rs, 1, 0)
                    hidden_t(0, rs + EV_MOE)
                    unit_out(MOE0 + 3, rs, 1, 1)
                if not first:
                    pe.wait_ge(h_added, 4 * prev + 4)
                gather(job + 1)
                pe.wait_ge(tlo_ready, r + EV_MOE + STEPS)
                for i in range(2):
                    unit_out(MOE0 + FFN_UNITS - 2 + i, r, 1, i, True)

            pe.wait_ge(nlo_ready, 2)
            pe.wait_ge(zero_set, 2)
            gather(0)
            expert()
            pe.wait_ge(table_ready, 1)
            more = pe.value_load(jobs_i[0:1, 0:1], min_val=NE - 1, max_val=JOBS - 1)
            with pe.Fori(0, more) as prev:
                expert(prev)
            pe.wait_ge(gxlo, 2 * more + 4)
            scatter(more)


_INS = ["x", "mem", "rel_bias_table", "mem_norm", "norm_mix", "norm_ffn", "final_norm", "swa_w_in", "swa_sinks",
        "swa_w_mem_kv", "swa_w_out", "dil_w_in", "dil_w_mem_kv", "dil_w_out", "ffn_gate", "ffn_up", "ffn_down",
        "router", "moe_gate", "moe_up", "moe_down"]


def kernel(**inputs):
    import concourse.bacc as bacc
    from concourse.bass_utils import run_bass_kernel_spmd

    nc = bacc.Bacc("TRN2", target_bir_lowering=False, num_devices=1)
    index_mats, bias_onehot = shape_constants()
    arrays = {name: np.ascontiguousarray(inputs[name]) for name in _INS}
    arrays["index_mats"], arrays["bias_onehot"] = index_mats, bias_onehot
    args = [nc.dram_tensor(f"in_{name}", a.shape, mybir.dt.from_np(a.dtype), kind="ExternalInput").ap()
            for name, a in arrays.items()]
    out = nc.dram_tensor("out_trunk", (1, SEQ, D), F32, kind="ExternalOutput").ap()
    trunk(nc, *args, out)
    result = run_bass_kernel_spmd(nc, [{f"in_{name}": a for name, a in arrays.items()}], core_ids=[0])
    return result.results[0]["out_trunk"]
```

```python
from contextlib import ExitStack

import numpy as np

import concourse.bass as bass
from concourse import mybir

F32 = mybir.dt.float32
F32R = mybir.dt.float32r
I32 = mybir.dt.int32
ACT = mybir.ActivationFunctionType
ALU = mybir.AluOpType
AX = mybir.AxisListType

P = 128
D = 1024
SEQ = 256
TILES = SEQ // P
KT = D // P
DFF = 3584
FCH = 512
STEPS = DFF // FCH
FT = FCH // P
NE = 8
HD = 64
NH = 12
MH = 4
ITEMS = NH + MH
NEG = -1e30
LOWEST = -3e38
EPS = 1e-5
RAW = 6
CUT = 3
UNIT = 2048
SWA_IN = 1408
DIL_IN = 2560
MAX_OVER = (2 * SEQ) // (P + 1)
JOBS = NE + MAX_OVER
COLS = JOBS + 1
RLEN = 3 * P

CHUNKS = (
    [("mk0", 512, 8, 0), ("mk1", 512, 8, 0)]
    + [("si", min(512, SWA_IN - o), 8, o) for o in range(0, SWA_IN, 512)]
    + [("so", 512, 8, o) for o in range(0, D, 512)]
    + [("di", 512, 8, o) for o in range(0, DIL_IN, 512)]
    + [("do", 512, 4, o) for o in range(0, D, 512)]
)
FFN_UNITS = STEPS * 6


def plan_units():
    first, n, ffn = [], 0, None
    for name, _, rows, _ in CHUNKS:
        if name == "di" and ffn is None:
            ffn, n = n, n + FFN_UNITS
        first.append(n)
        n += rows // 4
    return first, ffn, n


FIRST, FFN0, MOE0 = plan_units()
C_SI, C_SO, C_DI, C_DO = 2, 5, 7, 12
ACT_EV = [sum(CHUNKS[i][0] not in ("so", "do") for i in range(c + 1)) for c in range(len(CHUNKS))]
DVE_EV = [sum(2 if CHUNKS[i][0] in ("so", "do") else 1 for i in range(c + 1)) for c in range(len(CHUNKS))]
TR_BANKS = [4, 4, 4, 4, 4, 2, 4]
TR0 = [sum(TR_BANKS[:i]) for i in range(len(TR_BANKS) + 1)]
T_MEM, T_MIX0, T_CAT0, T_FFN0, T_MIX1, T_CAT1, T_ROUTE = range(7)
XT_FREE = [0, FIRST[C_SI], FIRST[C_SO], FFN0, FIRST[C_DI], FIRST[C_DO]]
EV_MOE = TILES * STEPS


def t5_bucket(dist):
    d = np.maximum(dist, 0)
    ratio = np.maximum(d, 1).astype(np.float32) / np.float32(16)
    large = 16 + (np.log(ratio).astype(np.float32) / np.float32(np.log(2048 / 16)) * 16).astype(np.int32)
    return np.where(d < 16, d, np.minimum(large, 31))


def shape_constants():
    c = np.zeros((P, 5 * P + 80), np.float32)
    i = np.arange(P)
    c[:, 0:P] = np.eye(P)
    c[:, P:2 * P] = np.eye(P)[::-1]
    c[:, 2 * P:3 * P] = i[:, None] < i[None, :]
    c[:, 3 * P:4 * P] = 1.0
    c[:, 4 * P:5 * P] = i[None, :]
    e = np.arange(NE)
    c[:, 5 * P:5 * P + 64] = (e[None, :] < e[:, None]).reshape(-1)
    c[:, 5 * P + 64] = EPS
    c[:, 5 * P + 65:5 * P + 73] = e
    dist = 2 * P - 1 - np.arange(RLEN)
    one = np.zeros((33, 4, RLEN), np.float32)
    b = t5_bucket(dist)
    for g, (most, dil) in enumerate([(127, 1), (128, 1), (512, 4), (2048, 16)]):
        one[b, g, np.arange(RLEN)] = 1.0
        ok = (dist >= 0) & (dist <= most) & (dist % dil == 0)
        one[32, g] = np.where(ok, 0.0, NEG)
    return c, one


def wait(eng, sem, value):
    if not isinstance(value, int) or value > 0:
        eng.wait_ge(sem, value)


def free(ap, *dims):
    return bass.AP(ap.tensor, ap.offset, [list(ap.ap[0])] + [list(d) for d in dims])


def trunk(nc, x, mem, rel_bias_table, mem_norm, norm_mix, norm_ffn, final_norm, swa_w_in, swa_sinks,
          swa_w_mem_kv, swa_w_out, dil_w_in, dil_w_mem_kv, dil_w_out, ffn_gate, ffn_up, ffn_down, router,
          moe_gate, moe_up, moe_down, index_mats, bias_onehot, out):
    chunk_w = {
        "mk0": swa_w_mem_kv, "mk1": dil_w_mem_kv, "si": swa_w_in, "so": swa_w_out, "di": dil_w_in, "do": dil_w_out,
    }
    chunk_w = {k: v.rearrange("z (k p) f -> p (z k) f", p=P) for k, v in chunk_w.items()}
    ffn_in = [w.rearrange("z (k p) f -> p (z k) f", p=P) for w in (ffn_up, ffn_gate)]
    ffn_out = ffn_down.rearrange("z (k p) f -> p (z k) f", p=P)
    moe_in = [w.rearrange("z e (k p) f -> p (z e) k f", p=P) for w in (moe_up, moe_gate)]
    moe_out = moe_down.rearrange("z e (k p) f -> p (z e) k f", p=P)
    gains = [mem_norm, norm_mix[0, :], norm_ffn[0, :], norm_mix[1, :], norm_ffn[1, :], final_norm]

    bias_rows = [nc.dram_tensor(f"bias_rows_{i}", (NH, RLEN), F32, kind="Internal").ap() for i in range(2)]

    ctx = ExitStack()
    with ctx:
        def sb(name, shape, dt=F32, scope=ctx):
            return scope.enter_context(nc.sbuf_tensor(name, shape, dt))

        def sem(name):
            return ctx.enter_context(nc.semaphore(name))

        raw = sb("raw", [P, RAW, UNIT])
        whi = sb("whi", [P, CUT, UNIT], F32R)
        wlo = sb("wlo", [P, CUT, UNIT], F32R)
        h = sb("h", [P, TILES, D])
        hn = sb("hn", [P, TILES, D])
        xhi = sb("xhi", [P, KT, SEQ], F32R)
        xlo = sb("xlo", [P, KT, SEQ], F32R)
        gain = sb("gain", [P, 2, D])
        memkv = sb("memkv", [P, 2, TILES, 512])
        mats = sb("mats", [P, 5 * P + 80])
        stats = sb("stats", [P, 64])
        squares = sb("squares", [P, D])
        ident, anti, before, ones, iota = (mats[:, i * P:(i + 1) * P] for i in range(5))
        tri, eps, expert_no = mats[:, 640:704], mats[:, 704:705], mats[:, 705:713]
        ssq, std, rstd = stats[:, 0:12], stats[:, 16:28], stats[:, 32:44]

        with ExitStack() as mix:
            proj = sb("proj", [P, TILES, DIL_IN], scope=mix)
            bias = sb("bias", [P, NH, SEQ], scope=mix)
            qk = sb("qk", [HD, 2, 512], scope=mix)
            probs = sb("probs", [P, 2, 512], scope=mix)
            probsT = sb("probsT", [P, 2, 512], scope=mix)
            oraw = sb("oraw", [P, TILES, ITEMS, HD], scope=mix)
            sm = sb("sm", [P, 512], scope=mix)
        with ExitStack() as glu:
            thi = sb("thi", [P, FT, SEQ], F32R, scope=glu)
            tlo = sb("tlo", [P, FT, SEQ], F32R, scope=glu)
            silu = sb("silu", [P, TILES, FCH], scope=glu)
            act_h = sb("act_h", [P, TILES, FCH], scope=glu)
            nhi = sb("nhi", [P, TILES, D], F32R, scope=glu)
            nlo = sb("nlo", [P, TILES, D], F32R, scope=glu)
            yhi = sb("yhi", [P, D], F32R, scope=glu)
            ylo = sb("ylo", [P, D], F32R, scope=glu)
            zero = sb("zero", [P, 512], F32R, scope=glu)
            pick = sb("pick", [P, TILES, P], F32R, scope=glu)
            put_next = sb("put_next", [P, SEQ], scope=glu)
            put = sb("put", [P, SEQ], F32R, scope=glu)
            gate_next = sb("gate_next", [P, 1], scope=glu)
            gate = sb("gate", [P, 1], scope=glu)
            rt = sb("rt", [P, 1024], scope=glu)
            rw = sb("rw", [P, KT, NE], scope=glu)
            pos = sb("pos", [P, TILES, COLS], scope=glu)
            comb = sb("comb", [P, TILES, COLS], scope=glu)
            jobs_i = sb("jobs_i", [1, 8], I32, scope=glu)
        with ExitStack() as early:
            sb("under_proj", [P, TILES, DIL_IN], scope=early)
            onehot = sb("onehot", [33, 4, RLEN], scope=early)
            table = sb("table", [33, NH], scope=early)
            rows = sb("rows", [NH, 4, RLEN], scope=early)
        xtf = memkv[:, :, :, :].rearrange("p l t c -> p (l t c)").rearrange("p (k t) -> p k t", k=KT)
        ps = ctx.enter_context(nc.psum_tensor("ps", [P, 8, 512], F32))

        x_in, const_in, out_done = sem("x_in"), sem("const_in"), sem("out_done")
        mem_in = [sem("mem_in0"), sem("mem_in1")]
        onehot_in, table_in, sink_in, rw_in = sem("onehot_in"), sem("table_in"), sem("sink_in"), sem("rw_in")
        gain_in, x_gain_in = [sem("gain_in0"), sem("gain_in1")], sem("x_gain_in")
        raw_full = [sem(f"raw_full{i}") for i in range(RAW)]
        hi_ready, lo_ready, units_done = sem("hi_ready"), sem("lo_ready"), sem("units_done")
        table_one, rows_mm, rows_sb, rows_out, bias_in = (
            sem("table_one"), sem("rows_mm"), sem("rows_sb"), sem("rows_out"), sem("bias_in"))
        sq_done, std_done, rstd_done, hn_done = sem("sq_done"), sem("std_done"), sem("rstd_done"), sem("hn_done")
        tr_done, xhi_ready, xlo_ready = sem("tr_done"), sem("xhi_ready"), sem("xlo_ready")
        chunk_done, ev_act, ev_dve, y0_done = sem("chunk_done"), sem("ev_act"), sem("ev_dve"), sem("y0_done")
        qkT_done, qk_ready, s_done, nmr_done, nm_ready = (
            sem("qkT_done"), sem("qk_ready"), sem("s_done"), sem("nmr_done"), sem("nm_ready"))
        p_ready, pT_done, pT_ready, o_done, o_out = (
            sem("p_ready"), sem("pT_done"), sem("pT_ready"), sem("o_done"), sem("o_out"))
        fexp_in, fexp_out, cat_done = sem("fexp_in"), sem("fexp_out"), sem("cat_done")
        dve_chain = sem("dve_chain")
        g_done, silu_ready, act_ready, t_done, thi_ready, tlo_ready = (
            sem("g_done"), sem("silu_ready"), sem("act_ready"), sem("t_done"), sem("thi_ready"), sem("tlo_ready"))
        zero_set, ffn_added = sem("zero_set"), sem("ffn_added")
        xtf_ready, logit_done, top_in, top_exp, rank_in, rank_done, comb_ready, table_ready = (
            sem("xtf_ready"), sem("logit_done"), sem("top_in"), sem("top_exp"), sem("rank_in"), sem("rank_done"),
            sem("comb_ready"), sem("table_ready"))
        nhi_ready, nlo_ready = sem("nhi_ready"), sem("nlo_ready")
        pick_ready, gx_done, put_done, gxhi, gxlo, put_out, put_now = (
            sem("pick_ready"), sem("gx_done"), sem("put_done"), sem("gxhi"), sem("gxlo"), sem("put_out"),
            sem("put_now"))
        yhi_ready, ylo_ready, sc_done, h_added = sem("yhi_ready"), sem("ylo_ready"), sem("sc_done"), sem("h_added")
        block = ctx.enter_context(nc.Block())

        items = [[], []]
        for i in range(NH):
            items[0].append((i * HD, 768 + i // 4 * HD, 960 + i // 4 * HD))
            base = i // 4 * 768 + i % 4 * HD
            items[1].append((base, base + 256, base + 512))
        for m in range(MH):
            items[0].append((1152 + m * HD, m * HD, 256 + m * HD))
            items[1].append((2304 + m * HD, m * HD, 256 + m * HD))

        def kv(layer, i, t, col):
            src = proj[:, t, col:col + HD] if i < NH else memkv[:, layer, t, col:col + HD]
            return src

        B_U, B_G, B_Y = (0, 1), (2, 3), ((4, 5), (6, 7))
        B_X, B_PUT, B_SC = (6, 7), 3, (1, 3, 6, 7)
        B_LG, B_RANK = (4, 6), 5

        def uses(c, rounds):
            return c // RAW + 1 + rounds

        def token_banks(op, t):
            n = TR_BANKS[op] // TILES
            return [(t * n + i, i) for i in range(n)]

        def part(x3, half, t):
            return x3[:, 4 * half:4 * half + 4, t * P:(t + 1) * P]

        def four(bank):
            return ps[:, bank, :].rearrange("p (k t) -> p k t", k=4)

        def span(c):
            for k, (_, width, rows_, _) in enumerate(CHUNKS):
                if FIRST[k] <= c < FIRST[k] + rows_ // 4:
                    return 4 * width
            return UNIT

        @block.sync
        def _(sp):
            for t in range(TILES):
                sp.dma_start(hn[:, t, :], mem[0, t * P:(t + 1) * P, :]).then_inc(mem_in[t], 16)

            def load(c, rounds, src):
                wait(sp, lo_ready, c + RAW * rounds - RAW + 1)
                dst = raw[:, c % RAW, 0:span(c)].rearrange("p (k f) -> p k f", k=src.shape[-2])
                sp.dma_start(dst, src).then_inc(raw_full[c % RAW], 16)

            def load_chunks(lo, hi):
                for k in range(lo, hi):
                    name, width, rows_, off = CHUNKS[k]
                    for i in range(rows_ // 4):
                        load(FIRST[k] + i, 0, chunk_w[name][:, 4 * i:4 * i + 4, off:off + width])

            load_chunks(0, 1)
            sp.dma_start(h[:, :, :], x[0].rearrange("(t p) d -> p t d", p=P)).then_inc(x_in, 16)
            sp.dma_start(gain[:, 1, :], bass.AP(gains[1].tensor, gains[1].offset, [[0, P], [1, D]]))\
                .then_inc(x_gain_in, 16)
            load_chunks(1, C_DI)
            for i in range(4):
                load(FFN0 + i, 0, ffn_in[i // 2][:, i % 2 * 4:i % 2 * 4 + 4, 0:FCH])
            with sp.Fori(1, STEPS) as s:
                for i in range(4):
                    load(FFN0 - 2 + i, s, ffn_in[i // 2][:, i % 2 * 4:i % 2 * 4 + 4, bass.ds(s * FCH, FCH)])
                for i in range(2):
                    load(FFN0 + 2 + i, s, ffn_out[:, bass.ds(s * FT - FT + 2 * i, 2), :])
            for i in range(2):
                load(FFN0 + FFN_UNITS - 2 + i, 0, ffn_out[:, (STEPS - 1) * FT + 2 * i:(STEPS - 1) * FT + 2 * i + 2, :])
            load_chunks(C_DI, len(CHUNKS))

            def load_expert(job, e):
                for i in range(4):
                    load(MOE0 + i, STEPS * job, moe_in[i // 2][:, bass.ds(e, 1), i % 2 * 4:i % 2 * 4 + 4, 0:FCH])
                with sp.Fori(1, STEPS) as s:
                    for i in range(4):
                        load(MOE0 - 2 + i, job * STEPS + s,
                             moe_in[i // 2][:, bass.ds(e, 1), i % 2 * 4:i % 2 * 4 + 4, bass.ds(s * FCH, FCH)])
                    for i in range(2):
                        load(MOE0 + 2 + i, job * STEPS + s,
                             moe_out[:, bass.ds(e, 1), bass.ds(s * FT - FT + 2 * i, 2), :])
                for i in range(2):
                    f = (STEPS - 1) * FT + 2 * i
                    load(MOE0 + FFN_UNITS - 2 + i, STEPS * job, moe_out[:, bass.ds(e, 1), f:f + 2, :])

            with sp.Fori(0, NE) as job:
                load_expert(job, job)
            sp.wait_ge(table_ready, 1)
            n_over = sp.value_load(jobs_i[0:1, 1:2], min_val=0, max_val=MAX_OVER)
            with sp.If(n_over > 0):
                with sp.Fori(0, n_over) as o:
                    e = sp.value_load(jobs_i[0:1, bass.ds(o + 2, 1)], min_val=0, max_val=NE - 1)
                    load_expert(o + NE, e)
            for t in range(TILES):
                sp.wait_ge(hn_done, 2 * 5 + t + 1)
                sp.dma_start(out[0, t * P:(t + 1) * P, :], hn[:, t, :]).then_inc(out_done, 16)
            sp.wait_ge(out_done, 16 * TILES)

        @block.gpsimd
        def _(pool):
            def load_gain(k):
                if k >= 2:
                    pool.wait_ge(hn_done, 2 * (k - 2) + 2)
                pool.dma_start(gain[:, k % 2, :], bass.AP(gains[k].tensor, gains[k].offset, [[0, P], [1, D]]))\
                    .then_inc(gain_in[k % 2], 16)

            load_gain(0)
            pool.dma_start(sm[:, 496:508], bass.AP(swa_sinks.tensor, swa_sinks.offset, [[0, P], [1, NH]]))\
                .then_inc(sink_in, 16)
            pool.wait_ge(rows_sb, 4)
            pool.dma_start(bias_rows[0], rows[0:NH, 0, :]).then_inc(rows_out, 16)
            for g in range(3):
                pool.dma_start(bias_rows[1][4 * g:4 * g + 4, :], rows[0:4, 1 + g, :]).then_inc(rows_out, 16)
            pool.wait_ge(rows_out, 64)

            def load_bias(layer):
                b = bias_rows[layer]
                for n in range(3):
                    src = bass.AP(b.tensor, b.offset + 4 * n * RLEN, [[1, P], [RLEN, 4], [1, SEQ]])
                    pool.dma_start(bias[:, 4 * n:4 * n + 4, :], src).then_inc(bias_in, 16)

            load_bias(0)
            load_gain(2)
            load_gain(3)
            pool.wait_ge(s_done, ITEMS)
            load_bias(1)
            load_gain(4)
            pool.wait_ge(cat_done, 4)
            pool.dma_start(rw[:, :, :], router[0].rearrange("(k p) e -> p k e", p=P)).then_inc(rw_in, 16)
            load_gain(5)

        @block.scalar
        def _(act):
            act.dma_start(mats[:, :], index_mats).then_inc(const_in, 16)

            nxt = [0]
            preloads = [0]

            def cut(c, rounds):
                act.wait_ge(raw_full[c % RAW], 16 * uses(c, rounds))
                wait(act, units_done, c + RAW * rounds - CUT + 1)
                act.activation(whi[:, c % CUT, 0:span(c)], raw[:, c % RAW, 0:span(c)], ACT.Copy).then_inc(hi_ready, 1)

            def cut_upto(n):
                while nxt[0] < n:
                    cut(nxt[0], 0)
                    nxt[0] += 1

            def preload(func):
                column = 48 + preloads[0]
                preloads[0] += 1
                act.activation(stats[:, column:column + 1], eps, func)

            def norm_root(k, t, src):
                wait(act, sq_done, 2 * k + t)
                act.activation(squares[:, :], src[:, t, :], ACT.Square,
                               accum_out=ssq[:, 2 * k + t:2 * k + t + 1]).then_inc(sq_done, 1)
                act.wait_ge(sq_done, 2 * k + t + 1)
                act.activation(std[:, 2 * k + t:2 * k + t + 1], ssq[:, 2 * k + t:2 * k + t + 1], ACT.Sqrt, bias=eps,
                               scale=1.0 / D).then_inc(std_done, 1)

            def xT_hi(op, t):
                if (op, t) != (T_MIX0, 0):
                    wait(act, units_done, XT_FREE[op])
                for b, half in token_banks(op, t):
                    act.wait_ge(tr_done, TR0[op] + b + 1)
                    act.activation(part(xhi, half, t), four(b), ACT.Copy).then_inc(xhi_ready, 1)

            def chunk_out(c, dst):
                cut_upto(FIRST[c] + CHUNKS[c][2] // 4 + 2)
                act.wait_ge(chunk_done, c + 1)
                act.activation(dst, ps[:, 4 + 2 * (c % 2), 0:CHUNKS[c][1]], ACT.Copy).then_inc(ev_act, 1)

            def attention(layer):
                base = ITEMS * layer
                for n in range(ITEMS + 1):
                    if n < ITEMS:
                        act.wait_ge(qkT_done, base + n + 1)
                        wait(act, s_done, base + n - 1)
                        act.activation(qk[:, n % 2, :], ps[0:HD, 0, :], ACT.Copy).then_inc(qk_ready, 1)
                    if n >= 1:
                        i = n - 1
                        bank = 3 + (base + i) % 3
                        act.wait_ge(nm_ready, base + i + 1)
                        if i >= NH:
                            act.wait_ge(pT_done, base + i - 1)
                        w0 = P if i < NH else SEQ
                        for qb, (a, b) in enumerate([(0, w0), (w0, w0 + SEQ)]):
                            scores = probs[:, i % 2, a:b] if i < NH else ps[:, bank, a:b]
                            act.activation(probs[:, i % 2, a:b], scores, ACT.Exp,
                                           bias=sm[:, 32 + 16 * qb + i:33 + 16 * qb + i], scale=0.125,
                                           accum_out=sm[:, 64 + 16 * qb + i:65 + 16 * qb + i]).then_inc(p_ready, 1)
                    if n == ITEMS - 1:
                        act.wait_ge(fexp_in, layer + 1)
                        w = 2 * TILES * NH if layer == 0 else TILES * NH
                        act.activation(sm[:, 128:128 + w], sm[:, 128:128 + w], ACT.Exp).then_inc(fexp_out, 1)

            def glu_silu(t, ev, signal, value):
                act.wait_ge(signal, value)
                act.activation(silu[:, t, :], ps[:, B_G[t], :], ACT.Silu).then_inc(silu_ready, 1)

            def glu_thi(t, ev, unit):
                act.wait_ge(t_done, ev + 1)
                wait(act, units_done, unit)
                act.activation(thi[:, :, t * P:(t + 1) * P], ps[:, B_G[t], :].rearrange("p (k t) -> p k t", k=FT),
                               ACT.Copy).then_inc(thi_ready, 1)

            act.wait_ge(const_in, 16)
            preload(ACT.Sqrt)
            for t in range(TILES):
                act.wait_ge(mem_in[t], 16)
                norm_root(0, t, hn)
            act.dma_start(onehot[:, :, :], bias_onehot).then_inc(onehot_in, 16)
            act.dma_start(table[0:32, :], rel_bias_table).then_inc(table_in, 16)
            for t in range(TILES):
                xT_hi(T_MEM, t)
                cut_upto(t + 1)
            act.wait_ge(x_in, 16)
            for t in range(TILES):
                norm_root(1, t, h)
            chunk_out(0, memkv[:, 0, 0, :])
            act.wait_ge(chunk_done, 2)
            xT_hi(T_MIX0, 0)
            chunk_out(1, memkv[:, 1, 0, :])
            xT_hi(T_MIX0, 1)
            chunk_out(C_SI, proj[:, 0, 0:CHUNKS[C_SI][1]])
            act.wait_ge(rows_mm, 1)
            for g in range(4):
                n = NH if g == 0 else 4
                act.activation(rows[0:n, g, :], ps[0:n, g, 0:RLEN], ACT.Copy, scale=8.0).then_inc(rows_sb, 1)
            preload(ACT.Exp)
            for c in range(C_SI + 1, C_SO):
                chunk_out(c, proj[:, 0, CHUNKS[c][3]:CHUNKS[c][3] + CHUNKS[c][1]])
            act.wait_ge(rows_out, 64)
            attention(0)
            for t in range(TILES):
                xT_hi(T_CAT0, t)
            preload(ACT.Sqrt)
            cut_upto(FFN0 + 1)
            for t in range(TILES):
                act.wait_ge(ev_dve, DVE_EV[C_SO + 1] - 1 + t)
                norm_root(2, t, h)
                cut_upto(FFN0 + 2)
                xT_hi(T_FFN0, t)
            preload(ACT.Silu)
            for i in range(4):
                cut(FFN0 + 2 + i, 0)
            glu_silu(0, 0, g_done, 1)
            glu_silu(1, 1, units_done, FFN0 + 4)
            for t in range(TILES):
                glu_thi(t, t, FFN0 + 4)
            with act.Fori(1, STEPS) as s:
                for i in range(4):
                    cut(FFN0 + i, s)
                glu_silu(0, s * TILES, g_done, s + 1)
                glu_silu(1, s * TILES + 1, units_done, s * 6 + FFN0 + 2)
                for i in range(2):
                    cut(FFN0 + 4 + i, s)
                for t in range(TILES):
                    glu_thi(t, s * TILES + t, FFN0 + 4 + 6 * s)
            nxt[0] = FFN0 + FFN_UNITS
            preload(ACT.Sqrt)
            cut_upto(FIRST[C_DI] + 1)
            for t in range(TILES):
                act.wait_ge(ffn_added, 2 * t + 2)
                norm_root(3, t, h)
                cut_upto(FIRST[C_DI] + 2)
                xT_hi(T_MIX1, t)
            preload(ACT.Exp)
            for c in range(C_DI, C_DO):
                chunk_out(c, proj[:, 0, CHUNKS[c][3]:CHUNKS[c][3] + CHUNKS[c][1]])
            attention(1)
            for t in range(TILES):
                xT_hi(T_CAT1, t)
            preload(ACT.Sqrt)
            cut_upto(MOE0 + 1)
            for t in range(TILES):
                act.wait_ge(ev_dve, DVE_EV[-1] - 2 + 2 * t)
                norm_root(4, t, h)
            cut_upto(MOE0 + 2)
            for t in range(TILES):
                for b, half in token_banks(T_ROUTE, t):
                    act.wait_ge(tr_done, TR0[T_ROUTE] + b + 1)
                    act.activation(part(xtf, half, t), four(b), ACT.Copy).then_inc(xtf_ready, 1)
            for t in range(TILES):
                act.wait_ge(hn_done, 9 + t)
                act.activation(nhi[:, t, :], hn[:, t, :], ACT.Copy).then_inc(nhi_ready, 1)
            preload(ACT.Exp)
            cut_upto(MOE0 + 3)
            act.wait_ge(top_in, 1)
            act.activation(rt[:, 160:176], rt[:, 160:176], ACT.Exp).then_inc(top_exp, 1)
            preload(ACT.Silu)

            def gather_hi(q):
                for b in range(2):
                    act.wait_ge(gx_done, 2 * q + b + 1)
                    act.activation(xhi[:, 4 * b:4 * b + 4, 0:P], four(B_X[b]), ACT.Copy).then_inc(gxhi, 1)

            def gather_put(q):
                act.wait_ge(put_done, q + 1)
                act.activation(put_next[:, :], ps[:, B_PUT, 0:SEQ], ACT.Copy).then_inc(put_out, 1)
                act.activation(gate_next[:, :], ps[:, B_PUT, SEQ:SEQ + 1], ACT.Copy).then_inc(put_out, 1)

            def y_hi(prev):
                act.wait_ge(units_done, prev * FFN_UNITS + FFN_UNITS + MOE0)
                for b in range(2):
                    act.activation(yhi[:, b * 512:(b + 1) * 512], ps[:, B_Y[0][b], :], ACT.Copy, scale=gate[:, 0:1])\
                        .then_inc(yhi_ready, 1)

            def expert(prev=None, final=False):
                first = prev is None
                job = 0 if first else prev + 1
                r = job * STEPS
                if first:
                    for i in range(3, 6):
                        cut(MOE0 + i, 0)
                    gather_put(0)
                else:
                    for i in range(2):
                        cut(MOE0 + i, r)
                    y_hi(prev)
                    for i in range(2, 6):
                        cut(MOE0 + i, r)
                glu_silu(0, r + EV_MOE, units_done, r * 6 + MOE0 + 4)
                if not first:
                    act.wait_ge(sc_done, 4 * prev + 4)
                act.wait_ge(put_out, 2 * job + 2)
                act.activation(put[:, :], put_next[:, :], ACT.Copy).then_inc(put_now, 1)
                act.activation(gate[:, :], gate_next[:, :], ACT.Copy).then_inc(put_now, 1)
                glu_thi(0, r + EV_MOE, r * 6 + MOE0 + 4)
                with act.Fori(1, STEPS) as s:
                    rs = s + job * STEPS
                    for i in range(4):
                        cut(MOE0 + i, rs)
                    glu_silu(0, rs + EV_MOE, units_done, rs * 6 + MOE0 + 2)
                    for i in range(2):
                        cut(MOE0 + 4 + i, rs)
                    glu_thi(0, rs + EV_MOE, rs * 6 + MOE0 + 4)
                if not final:
                    gather_hi(job + 1)
                    gather_put(job + 1)

            gather_hi(0)
            expert()
            act.wait_ge(table_ready, 1)
            middle = act.value_load(jobs_i[0:1, 0:1], min_val=NE - 2, max_val=JOBS - 2)
            with act.Fori(0, middle) as prev:
                expert(prev)
            expert(middle, True)
            preload(ACT.Sqrt)
            y_hi(middle + 1)
            for t in range(TILES):
                act.wait_ge(h_added, 4 * middle + 6 + 2 * t)
                norm_root(5, t, h)

        @block.vector
        def _(dve):
            nxt = [0]
            chain = [0]

            def link(ins):
                chain[0] += 1
                ins.then_inc(dve_chain, 1)
                dve.wait_ge(dve_chain, chain[0])

            def cut(c, rounds):
                dve.wait_ge(hi_ready, c + RAW * rounds + 1)
                n = span(c)
                dve.tensor_tensor(wlo[:, c % CUT, 0:n], raw[:, c % RAW, 0:n], whi[:, c % CUT, 0:n].bitcast(F32),
                                  ALU.subtract).then_inc(lo_ready, 1)

            def cut_upto(n):
                while nxt[0] < n:
                    cut(nxt[0], 0)
                    nxt[0] += 1

            def norm(k, t, src):
                dve.wait_ge(std_done, 2 * k + t + 1)
                dve.reciprocal(rstd[:, 2 * k + t:2 * k + t + 1], std[:, 2 * k + t:2 * k + t + 1]).then_inc(rstd_done, 1)
                dve.wait_ge(rstd_done, 2 * k + t + 1)
                if k == 1:
                    dve.wait_ge(x_gain_in, 16)
                else:
                    dve.wait_ge(gain_in[k % 2], 16 * (k // 2 + 1 - k % 2))
                dve.scalar_tensor_tensor(hn[:, t, :], src[:, t, :], rstd[:, 2 * k + t:2 * k + t + 1],
                                         gain[:, k % 2, :], ALU.mult, ALU.mult).then_inc(hn_done, 1)

            def xT_lo(op, t):
                for b, half in token_banks(op, t):
                    dve.wait_ge(xhi_ready, TR0[op] + b + 1)
                    dve.tensor_tensor(part(xlo, half, t), four(b), part(xhi, half, t).bitcast(F32), ALU.subtract)\
                        .then_inc(xlo_ready, 1)

            def chunk_out(c, dst):
                cut_upto(FIRST[c] + CHUNKS[c][2] // 4 + 2)
                dve.wait_ge(units_done, FIRST[c] + CHUNKS[c][2] // 4)
                dve.tensor_copy(dst, ps[:, 5 + 2 * (c % 2), 0:CHUNKS[c][1]]).then_inc(ev_dve, 1)

            def chunk_add(c, t):
                cols = slice(CHUNKS[c][3], CHUNKS[c][3] + 512)
                if t == 0:
                    dve.wait_ge(chunk_done, c + 1)
                else:
                    dve.wait_ge(units_done, FIRST[c] + CHUNKS[c][2] // 4)
                dve.tensor_tensor(h[:, t, cols], h[:, t, cols], ps[:, 4 + 2 * (c % 2) + t, :], ALU.add)\
                    .then_inc(ev_dve, 1)

            nm = sm[:, 32:64].rearrange("p (q i) -> p q i", q=2)
            den = sm[:, 64:96].rearrange("p (q i) -> p q i", q=2)
            wts = sm[:, 96:128].rearrange("p (q i) -> p q i", q=2)

            def attention(layer, factors, weights):
                base = ITEMS * layer
                for n in range(1, ITEMS + 2):
                    i = n - 1
                    if i < ITEMS:
                        dve.wait_ge(s_done, base + i + 1)
                        bank = 3 + (base + i) % 3
                        w0 = P if i < NH else SEQ
                        if i < NH:
                            wait(dve, pT_done, base + i - 1)
                            if i == 0:
                                dve.wait_ge(bias_in, 48 * (layer + 1))
                        for qb, (a, b) in enumerate([(0, w0), (w0, w0 + SEQ)]):
                            most = sm[:, 16 * qb + i:16 * qb + i + 1]
                            if i < NH:
                                last = dve.tensor_tensor_reduce(probs[:, i % 2, a:b], ps[:, bank, a:b],
                                                                bias[:, i, SEQ - (b - a):SEQ], 1.0, LOWEST,
                                                                ALU.add, ALU.max, most)
                            else:
                                last = dve.tensor_reduce(most, ps[:, bank, a:b], AX.X, ALU.max)
                            last.then_inc(nmr_done, 1)
                        dve.wait_ge(nmr_done, 2 * (base + i + 1))
                        dve.tensor_scalar(free(sm[:, 32 + i:33 + i], (16, 2)), free(sm[:, i:i + 1], (16, 2)), -0.125,
                                          None, ALU.mult).then_inc(nm_ready, 1)
                    i = n - 2
                    if 0 <= i < ITEMS:
                        dve.wait_ge(pT_done, base + i + 1)
                        wait(dve, o_done, base + i - 1)
                        w = 384 if i < NH else 512
                        dve.tensor_copy(probsT[:, i % 2, 0:w], ps[:, 1 + (base + i) % 2, 0:w]).then_inc(pT_ready, 1)
                    if n in (6, 10, 14):
                        g = (n - 6) // 4
                        dve.wait_ge(o_done, 4 * (4 * layer + g + 1))
                        dve.tensor_copy(oraw[:, :, 4 * g:4 * g + 4, :].rearrange("p q i d -> p q (i d)"),
                                        ps[:, 6 + g % 2, :].rearrange("p (q c) -> p q c", q=2)).then_inc(o_out, 1)
                    if n == ITEMS - 1:
                        factors()
                    if n == ITEMS:
                        weights()
                link(dve.reciprocal(wts[:, :, NH:], den[:, :, NH:]))

            def memory_out(layer, t, dst):
                dve.wait_ge(o_done, 4 * (4 * layer + 4))
                dve.tensor_tensor(dst.rearrange("p (i d) -> p i d", i=MH),
                                  ps[:, 7, t * SEQ:(t + 1) * SEQ].rearrange("p (i d) -> p i d", i=MH),
                                  free(sm[:, 108 + 16 * t:109 + 16 * t], (1, MH), (0, HD)), ALU.mult)\
                    .then_inc(cat_done, 1)

            def factors0():
                f = sm[:, 128:152].rearrange("p (q i) -> p q i", q=2)
                es = sm[:, 152:176].rearrange("p (q i) -> p q i", q=2)
                nm2 = sm[:, 176:200].rearrange("p (q i) -> p q i", q=2)
                sink2 = free(sm[:, 256:257], (0, 2), (1, NH))
                dve.wait_ge(sink_in, 16)
                link(dve.tensor_scalar(sm[:, 256:268], sm[:, 496:508], -1.0, None, ALU.mult))
                link(dve.tensor_tensor(nm2, nm[:, :, 0:NH], sink2, ALU.min))
                dve.tensor_tensor(f, nm2, nm[:, :, 0:NH], ALU.subtract)
                dve.tensor_tensor(es, nm2, sink2, ALU.subtract).then_inc(fexp_in, 1)

            def weights0():
                f = sm[:, 128:152].rearrange("p (q i) -> p q i", q=2)
                es = sm[:, 152:176].rearrange("p (q i) -> p q i", q=2)
                tmp = sm[:, 200:224].rearrange("p (q i) -> p q i", q=2)
                dve.wait_ge(fexp_out, 1)
                link(dve.tensor_tensor(tmp, f, den[:, :, 0:NH], ALU.mult))
                link(dve.tensor_tensor(tmp, tmp, es, ALU.add))
                link(dve.reciprocal(tmp, tmp))
                link(dve.tensor_tensor(wts[:, :, 0:NH], f, tmp, ALU.mult))

            def factors1():
                f = sm[:, 128:152].rearrange("p (q g i) -> p q g i", q=2, g=3)
                low = sm[:, 176:184].rearrange("p (q i) -> p q i", q=2)
                link(dve.tensor_tensor(low, nm[:, :, 0:4], nm[:, :, 4:8], ALU.min))
                link(dve.tensor_tensor(low, low, nm[:, :, 8:12], ALU.min))
                for g in range(3):
                    last = dve.tensor_tensor(f[:, :, g, :], low, nm[:, :, 4 * g:4 * g + 4], ALU.subtract)
                last.then_inc(fexp_in, 1)

            def weights1():
                f = sm[:, 128:152].rearrange("p (q g i) -> p q g i", q=2, g=3)
                tmp = sm[:, 200:224].rearrange("p (q g i) -> p q g i", q=2, g=3)
                tot = sm[:, 184:192].rearrange("p (q i) -> p q i", q=2)
                dve.wait_ge(fexp_out, 2)
                link(dve.tensor_tensor(sm[:, 200:224].rearrange("p (q i) -> p q i", q=2),
                                       sm[:, 128:152].rearrange("p (q i) -> p q i", q=2), den[:, :, 0:NH], ALU.mult))
                link(dve.tensor_tensor(tot, tmp[:, :, 0, :], tmp[:, :, 1, :], ALU.add))
                link(dve.tensor_tensor(tot, tot, tmp[:, :, 2, :], ALU.add))
                link(dve.reciprocal(tot, tot))
                for g in range(3):
                    last = dve.tensor_tensor(wts[:, :, 4 * g:4 * g + 4], f[:, :, g, :], tot, ALU.mult)
                link(last)

            def glu_mul(t, ev):
                dve.wait_ge(silu_ready, ev + 1)
                dve.tensor_tensor(act_h[:, t, :], ps[:, B_U[t], :], silu[:, t, :], ALU.mult).then_inc(act_ready, 1)

            def glu_tlo(t, ev):
                dve.wait_ge(thi_ready, ev + 1)
                dve.tensor_tensor(tlo[:, :, t * P:(t + 1) * P], ps[:, B_G[t], :].rearrange("p (k t) -> p k t", k=FT),
                                  thi[:, :, t * P:(t + 1) * P].bitcast(F32), ALU.subtract).then_inc(tlo_ready, 1)

            dve.memset(table[32:33, :], 1.0).then_inc(table_one, 1)
            for t in range(TILES):
                norm(0, t, hn)
            for t in range(TILES):
                xT_lo(T_MEM, t)
                cut_upto(t + 1)
            for t in range(TILES):
                norm(1, t, h)
            chunk_out(0, memkv[:, 0, 1, :])
            xT_lo(T_MIX0, 0)
            chunk_out(1, memkv[:, 1, 1, :])
            xT_lo(T_MIX0, 1)
            for c in range(C_SI, C_SO):
                chunk_out(c, proj[:, 1, CHUNKS[c][3]:CHUNKS[c][3] + CHUNKS[c][1]])
            attention(0, factors0, weights0)
            for t in range(TILES):
                dve.tensor_tensor(hn[:, t, 0:NH * HD].rearrange("p (i d) -> p i d", i=NH), oraw[:, t, 0:NH, :],
                                  free(sm[:, 96 + 16 * t:97 + 16 * t], (1, NH), (0, HD)), ALU.mult)
                memory_out(0, t, hn[:, t, NH * HD:])
            for t in range(TILES):
                xT_lo(T_CAT0, t)
            cut_upto(FIRST[C_SO + 1] + 2)
            for t in range(TILES):
                chunk_add(C_SO, t)
            cut_upto(FFN0 + 1)
            chunk_add(C_SO + 1, 0)
            norm(2, 0, h)
            chunk_add(C_SO + 1, 1)
            xT_lo(T_FFN0, 0)
            norm(2, 1, h)
            cut_upto(FFN0 + 2)
            xT_lo(T_FFN0, 1)
            dve.memset(zero[:, :].bitcast(F32), 0.0).then_inc(zero_set, 1)
            for i in range(4):
                cut(FFN0 + 2 + i, 0)
            for t in range(TILES):
                glu_mul(t, t)
            for t in range(TILES):
                glu_tlo(t, t)
            with dve.Fori(1, STEPS) as s:
                for i in range(4):
                    cut(FFN0 + i, s)
                for t in range(TILES):
                    glu_mul(t, s * TILES + t)
                for i in range(2):
                    cut(FFN0 + 4 + i, s)
                for t in range(TILES):
                    glu_tlo(t, s * TILES + t)
            nxt[0] = FFN0 + FFN_UNITS
            cut_upto(FIRST[C_DI] + 1)

            def ffn_add(t):
                if t == 0:
                    dve.wait_ge(y0_done, 1)
                else:
                    dve.wait_ge(units_done, FFN0 + FFN_UNITS)
                for b in range(2):
                    dve.tensor_tensor(h[:, t, b * 512:(b + 1) * 512], h[:, t, b * 512:(b + 1) * 512],
                                      ps[:, B_Y[t][b], :], ALU.add).then_inc(ffn_added, 1)

            ffn_add(0)
            norm(3, 0, h)
            ffn_add(1)
            xT_lo(T_MIX1, 0)
            norm(3, 1, h)
            cut_upto(FIRST[C_DI] + 2)
            xT_lo(T_MIX1, 1)
            for c in range(C_DI, C_DO):
                chunk_out(c, proj[:, 1, CHUNKS[c][3]:CHUNKS[c][3] + CHUNKS[c][1]])
            attention(1, factors1, weights1)
            for t in range(TILES):
                link(dve.tensor_tensor(oraw[:, t, 0:NH, :], oraw[:, t, 0:NH, :],
                                       free(sm[:, 96 + 16 * t:97 + 16 * t], (1, NH), (0, HD)), ALU.mult))
                o = oraw[:, t, :, :].rearrange("p i d -> p (i d)")
                link(dve.tensor_tensor(hn[:, t, 0:256], o[:, 0:256], o[:, 256:512], ALU.add))
                dve.tensor_tensor(hn[:, t, 0:256], hn[:, t, 0:256], o[:, 512:NH * HD], ALU.add)
                memory_out(1, t, hn[:, t, 256:512])
            for t in range(TILES):
                xT_lo(T_CAT1, t)
            chunk_add(C_DO, 0)
            chunk_add(C_DO + 1, 0)
            norm(4, 0, h)
            cut_upto(MOE0 + 1)
            chunk_add(C_DO, 1)
            chunk_add(C_DO + 1, 1)
            norm(4, 1, h)
            cut_upto(MOE0 + 2)

            dve.memset(zero[:, :].bitcast(F32), 0.0).then_inc(zero_set, 1)
            dve.memset(pos[:, :, :], -1.0)
            link(dve.memset(comb[:, :, :], 0.0))

            def n_lo(t):
                dve.wait_ge(nhi_ready, t + 1)
                dve.tensor_tensor(nlo[:, t, :], hn[:, t, :], nhi[:, t, :].bitcast(F32), ALU.subtract)\
                    .then_inc(nlo_ready, 1)

            l3 = rt[:, 0:16].rearrange("p (t e) -> p t e", t=2)
            gt, eq = rt[:, 32:160], rt[:, 192:320]
            ex = rt[:, 160:176].rearrange("p (t e) -> p t e", t=2)
            rank, sel = rt[:, 320:336], rt[:, 336:352]
            top, tot = rt[:, 352:354], rt[:, 354:356]
            tri3 = tri.rearrange("p (e f) -> p e f", e=NE)
            n_lo(0)
            dve.wait_ge(logit_done, 1)
            link(dve.tensor_copy(l3, free(ps[:, B_LG[0], 0:1], (512 * (B_LG[1] - B_LG[0]), 2), (1, NE))))
            other = free(rt[:, 0:1], (NE, 2), (0, NE), (1, NE))
            own = free(rt[:, 0:1], (NE, 2), (1, NE), (0, NE))
            cube = [free(a[:, 0:1], (64, 2), (NE, NE), (1, NE)) for a in (gt, eq)]
            dve.tensor_tensor(cube[0], other, own, ALU.is_gt)
            link(dve.tensor_tensor(cube[1], other, own, ALU.is_equal))
            link(dve.tensor_tensor(eq.rearrange("p (t c) -> p t c", t=2), eq.rearrange("p (t c) -> p t c", t=2),
                                   free(tri[:, 0:1], (0, 2), (1, 64)), ALU.mult))
            link(dve.tensor_tensor(gt, gt, eq, ALU.add))
            dve.tensor_reduce(top, l3, AX.X, ALU.max)
            link(dve.tensor_reduce(rank, gt.rearrange("p (t f) -> p t f", f=NE), AX.X, ALU.add))
            dve.tensor_scalar(sel, rank, 2.0, None, ALU.is_lt).then_inc(rank_in, 1)
            dve.tensor_tensor(ex, l3, free(top, (1, 2), (0, NE)), ALU.subtract).then_inc(top_in, 1)
            n_lo(1)
            dve.wait_ge(rank_in, 1)
            dve.wait_ge(rank_done, 1)
            p1 = rt[:, 368:384].rearrange("p (t e) -> p t e", t=2)
            over = rt[:, 384:392]
            link(dve.scalar_tensor_tensor(rt[:, 368:384], ps[:, B_RANK, 0:16], 1.0, sel, ALU.add, ALU.mult))
            link(dve.tensor_scalar(pos[:, :, 0:NE], p1, -1.0, None, ALU.add))
            for t in range(TILES):
                dve.tensor_scalar(pick[:, t, :], iota, pos[:, t, 0:1], None, ALU.is_equal).then_inc(pick_ready, 1)

            def combine_gates():
                dve.wait_ge(top_exp, 1)
                link(dve.tensor_tensor(ex, ex, sel.rearrange("p (t e) -> p t e", t=2), ALU.mult))
                link(dve.tensor_reduce(tot, ex, AX.X, ALU.add))
                link(dve.reciprocal(tot, tot))
                link(dve.tensor_tensor(comb[:, :, 0:NE], ex, free(tot, (1, 2), (0, NE)), ALU.mult))
                dve.tensor_scalar(over, ps[:, B_RANK, 16:24], float(P), None, ALU.is_gt).then_inc(comb_ready, 1)

            def table_of_jobs():
                dve.wait_ge(comb_ready, 1)
                om = rt[:, 400:464].rearrange("p (e f) -> p e f", e=NE)
                link(dve.tensor_tensor(om, free(over, (0, NE), (1, NE)), tri3, ALU.mult))
                link(dve.tensor_reduce(rt[:, 392:400], om, AX.X, ALU.add))
                oh = rt[:, 464:464 + NE * MAX_OVER]
                for o in range(MAX_OVER):
                    last = dve.scalar_tensor_tensor(oh[:, NE * o:NE * o + NE], rt[:, 392:400], float(o), over,
                                                    ALU.is_equal, ALU.mult)
                link(last)
                oh3 = oh.rearrange("p (o e) -> p o e", e=NE)
                pr = rt[:, 512:512 + NE * MAX_OVER].rearrange("p (o e) -> p o e", e=NE)
                red = rt[:, 560:560 + MAX_OVER]
                for t in range(TILES):
                    link(dve.tensor_tensor(pr, oh3, free(rt[:, 368 + 8 * t:369 + 8 * t], (0, MAX_OVER), (1, NE)),
                                           ALU.mult))
                    link(dve.tensor_reduce(red, pr, AX.X, ALU.add))
                    link(dve.tensor_scalar(pos[:, t, NE:JOBS], red, -1.0 - P, None, ALU.add))
                    link(dve.tensor_tensor(pr, oh3, free(comb[:, t, 0:1], (0, MAX_OVER), (1, NE)), ALU.mult))
                    link(dve.tensor_reduce(comb[:, t, NE:JOBS], pr, AX.X, ALU.add))
                link(dve.tensor_tensor(pr, oh3, free(expert_no, (0, MAX_OVER), (1, NE)), ALU.mult))
                dve.tensor_reduce(rt[:, 570:570 + MAX_OVER], pr, AX.X, ALU.add)
                link(dve.tensor_reduce(rt[:, 569:570], over, AX.X, ALU.add))
                link(dve.tensor_scalar(rt[:, 568:569], rt[:, 569:570], NE - 2.0, None, ALU.add))
                dve.tensor_copy(jobs_i[0:1, 0:2 + MAX_OVER], rt[0:1, 568:570 + MAX_OVER]).then_inc(table_ready, 1)

            def build_pick(q):
                wait(dve, put_done, q)
                for t in range(TILES):
                    dve.tensor_scalar(pick[:, t, :], iota, pos[:, t, bass.ds(q, 1)], None, ALU.is_equal)\
                        .then_inc(pick_ready, 1)

            def gather_lo(q):
                for b in range(2):
                    dve.wait_ge(gxhi, 2 * q + b + 1)
                    dve.tensor_tensor(xlo[:, 4 * b:4 * b + 4, 0:P], four(B_X[b]),
                                      xhi[:, 4 * b:4 * b + 4, 0:P].bitcast(F32), ALU.subtract).then_inc(gxlo, 1)

            def y_lo(prev):
                for b in range(2):
                    dve.wait_ge(yhi_ready, 2 * prev + 1 + b)
                    dve.scalar_tensor_tensor(ylo[:, b * 512:(b + 1) * 512], ps[:, B_Y[0][b], :], gate[:, 0:1],
                                             yhi[:, b * 512:(b + 1) * 512].bitcast(F32), ALU.mult, ALU.subtract)\
                        .then_inc(ylo_ready, 1)

            def add_scattered(prev):
                for n in range(4):
                    dve.wait_ge(sc_done, 4 * prev + 1 + n)
                    t, b = n // 2, n % 2
                    dve.tensor_tensor(h[:, t, b * 512:(b + 1) * 512], h[:, t, b * 512:(b + 1) * 512],
                                      ps[:, B_SC[n], :], ALU.add).then_inc(h_added, 1)

            def expert(prev=None, final=False):
                first = prev is None
                job = 0 if first else prev + 1
                r = job * STEPS
                if first:
                    table_of_jobs()
                    for i in range(3, 6):
                        cut(MOE0 + i, 0)
                    glu_mul(0, EV_MOE)
                    build_pick(1)
                else:
                    for i in range(2):
                        cut(MOE0 + i, r)
                    y_lo(prev)
                    if not final:
                        build_pick(job + 1)
                    for i in range(2, 6):
                        cut(MOE0 + i, r)
                    glu_mul(0, r + EV_MOE)
                    add_scattered(prev)
                glu_tlo(0, r + EV_MOE)
                with dve.Fori(1, STEPS) as s:
                    rs = s + job * STEPS
                    for i in range(4):
                        cut(MOE0 + i, rs)
                    glu_mul(0, rs + EV_MOE)
                    for i in range(2):
                        cut(MOE0 + 4 + i, rs)
                    glu_tlo(0, rs + EV_MOE)
                if not final:
                    gather_lo(job + 1)

            cut_upto(MOE0 + 3)
            combine_gates()
            gather_lo(0)
            expert()
            dve.wait_ge(table_ready, 1)
            middle = dve.value_load(jobs_i[0:1, 0:1], min_val=NE - 2, max_val=JOBS - 2)
            with dve.Fori(0, middle) as prev:
                expert(prev)
            expert(middle, True)
            y_lo(middle + 1)
            add_scattered(middle + 1)
            for t in range(TILES):
                norm(5, t, h)

        @block.tensor
        def _(pe):
            def three(dst, ahi, alo, bhi, blo, start, stop):
                pe.matmul(dst, ahi, bhi, start=start, stop=False)
                pe.matmul(dst, ahi, blo, start=False, stop=False)
                return pe.matmul(dst, alo, bhi, start=False, stop=stop)

            def transpose_x(op, t):
                turned = op in (T_CAT0, T_CAT1)
                for b, half in token_banks(op, t):
                    for j in range(4):
                        kt = 4 * half + j
                        dst, src = ps[:, b, j * P:(j + 1) * P], hn[:, t, kt * P:(kt + 1) * P]
                        if turned:
                            last = pe.matmul(dst, src, anti, start=True, stop=True)
                        else:
                            last = pe.transpose(dst, src, ident)
                    last.then_inc(tr_done, 1)

            def norm_transposed(k, op, t):
                pe.wait_ge(hn_done, 2 * k + t + 1)
                transpose_x(op, t)

            def chunk(c, op=None, between=None):
                _, width, rows_, _ = CHUNKS[c]
                if c >= 2:
                    pe.wait_ge(ev_act, ACT_EV[c - 2])
                    pe.wait_ge(ev_dve, DVE_EV[c - 2])
                n_units = rows_ // 4
                if op is None:
                    order = [(i, t) for i in range(n_units) for t in range(TILES)]
                else:
                    order = [(i, t) for t in range(TILES) for i in range(n_units)]
                for step, (i, t) in enumerate(order):
                    u = FIRST[c] + i
                    pe.wait_ge(lo_ready, u + 1)
                    if op is not None:
                        pe.wait_ge(xlo_ready, TR0[op] + t * n_units + i + 1)
                    dst = ps[:, 4 + 2 * (c % 2) + t, 0:width]
                    for j in range(4):
                        kt = 4 * i + j
                        cols = slice(j * width, (j + 1) * width)
                        last = three(dst, xhi[:, kt, t * P:(t + 1) * P], xlo[:, kt, t * P:(t + 1) * P],
                                     whi[:, u % CUT, cols], wlo[:, u % CUT, cols], kt == 0, kt == 4 * n_units - 1)
                    if t == TILES - 1:
                        last.then_inc(units_done, 1)
                    elif i == n_units - 1:
                        last.then_inc(chunk_done, 1)
                    if step == 0 and between is not None:
                        between()

            def attention(layer):
                base = ITEMS * layer
                for n in range(ITEMS + 3):
                    if n < ITEMS:
                        q, k, _ = items[layer][n]
                        wait(pe, qk_ready, base + n)
                        for t in range(TILES):
                            pe.matmul(ps[0:HD, 0, t * P:(t + 1) * P], proj[:, t, q:q + HD], anti, start=True,
                                      stop=True)
                        for t in range(TILES):
                            last = pe.transpose(ps[0:HD, 0, SEQ + t * P:SEQ + (t + 1) * P], kv(layer, n, t, k), ident)
                        last.then_inc(qkT_done, 1)
                    i = n - 1
                    if 0 <= i < ITEMS:
                        pe.wait_ge(qk_ready, base + i + 1)
                        wait(pe, p_ready, 2 * (base + i - 2))
                        bank = 3 + (base + i) % 3
                        w0 = P if i < NH else SEQ
                        for qb in range(TILES):
                            nk = w0 if qb == 0 else SEQ
                            dst = ps[:, bank, qb * w0:qb * w0 + nk]
                            last = pe.matmul(dst, qk[:, i % 2, qb * P:(qb + 1) * P], qk[:, i % 2, SEQ:SEQ + nk],
                                             start=True, stop=True)
                        last.then_inc(s_done, 1)
                    i = n - 2
                    if 0 <= i < ITEMS:
                        pe.wait_ge(p_ready, 2 * (base + i + 1))
                        wait(pe, pT_ready, base + i - 1)
                        for j in range(3 if i < NH else 4):
                            last = pe.transpose(ps[:, 1 + (base + i) % 2, j * P:(j + 1) * P],
                                                probs[:, i % 2, j * P:(j + 1) * P], ident)
                        last.then_inc(pT_done, 1)
                    i = n - 3
                    if 0 <= i < ITEMS:
                        pe.wait_ge(pT_ready, base + i + 1)
                        wait(pe, o_out, 3 * layer + max(i // 4 - 1, 0))
                        v = items[layer][i][2]
                        blocks = [[0], [0, 1]] if i < NH else [[0, 1], [0, 1]]
                        j = 0
                        for qb in range(TILES):
                            for m in blocks[qb]:
                                c0 = qb * SEQ + i % 4 * HD
                                last = pe.matmul(ps[:, 6 + (base + i) // 4 % 2, c0:c0 + HD],
                                                 probsT[:, i % 2, j * P:(j + 1) * P], kv(layer, i, m, v),
                                                 start=m == 0, stop=m == blocks[qb][-1])
                                j += 1
                        last.then_inc(o_done, 1)

            def in_tile(c, rounds, t, bank, half):
                for j in range(4):
                    kt = 4 * half + j
                    cols = slice(j * FCH, (j + 1) * FCH)
                    last = three(ps[:, bank[t], :], xhi[:, kt, t * P:(t + 1) * P], xlo[:, kt, t * P:(t + 1) * P],
                                 whi[:, c % CUT, cols], wlo[:, c % CUT, cols], kt == 0, kt == KT - 1)
                return last

            def unit_in(c, rounds, tiles, bank, half, first_tile_done=None):
                pe.wait_ge(lo_ready, c + RAW * rounds + 1)
                for t in range(tiles):
                    last = in_tile(c, rounds, t, bank, half)
                    if first_tile_done is not None and t == 0:
                        last.then_inc(first_tile_done, 1)
                last.then_inc(units_done, 1)

            def out_tile(c, t, half, final):
                for j in range(2):
                    ft = 2 * half + j
                    for b in range(2):
                        cols = slice(j * D + b * 512, j * D + b * 512 + 512)
                        last = three(ps[:, B_Y[t][b], :], thi[:, ft, t * P:(t + 1) * P],
                                     tlo[:, ft, t * P:(t + 1) * P], whi[:, c % CUT, cols], wlo[:, c % CUT, cols],
                                     False, final and half == 1 and j == 1)
                return last

            def unit_out(c, rounds, tiles, half, final=False):
                pe.wait_ge(lo_ready, c + RAW * rounds + 1)
                for t in range(tiles):
                    last = out_tile(c, t, half, final)
                last.then_inc(units_done, 1)

            def hidden_t(t, ev):
                pe.wait_ge(act_ready, ev + 1)
                for j in range(FT):
                    last = pe.transpose(ps[:, B_G[t], j * P:(j + 1) * P], act_h[:, t, j * P:(j + 1) * P], ident)
                last.then_inc(t_done, 1)

            def products_in(c, rounds, tiles, ev=None):
                for i in range(2):
                    unit_in(c + i, rounds, tiles, B_U, i)
                if ev is not None:
                    pe.wait_ge(tlo_ready, ev)
                unit_in(c + 2, rounds, tiles, B_G, 0)
                unit_in(c + 3, rounds, tiles, B_G, 1, g_done if tiles > 1 else None)

            def clear_y(tiles):
                for t in range(tiles):
                    for b in range(2):
                        pe.matmul(ps[:, B_Y[t][b], :], zero[:, 0:P], zero[:, :], start=True, stop=False)

            pe.wait_ge(const_in, 16)
            for t in range(TILES):
                norm_transposed(0, T_MEM, t)
            chunk(0, T_MEM)

            def x_transposed():
                for t in range(TILES):
                    norm_transposed(1, T_MIX0, t)

            chunk(1, T_MEM, x_transposed)
            chunk(C_SI, T_MIX0)
            pe.wait_ge(onehot_in, 16)
            pe.wait_ge(table_in, 16)
            pe.wait_ge(table_one, 1)
            for g in range(4):
                n = NH if g == 0 else 4
                heads = table[:, 0:NH] if g == 0 else table[:, 4 * g - 4:4 * g]
                last = pe.matmul(ps[0:n, g, 0:RLEN], heads, onehot[:, g, :], start=True, stop=True)
            last.then_inc(rows_mm, 1)
            for c in range(C_SI + 1, C_SO):
                chunk(c)
            pe.wait_ge(rows_sb, 4)
            pe.wait_ge(ev_act, ACT_EV[C_SO - 1])
            pe.wait_ge(ev_dve, DVE_EV[C_SO - 1])
            attention(0)
            def mixed_transposed(layer, op, t):
                pe.wait_ge(cat_done, 2 * layer + t + 1)
                transpose_x(op, t)

            mixed_transposed(0, T_CAT0, 0)
            chunk(C_SO, T_CAT0, lambda: mixed_transposed(0, T_CAT0, 1))
            chunk(C_SO + 1)
            norm_transposed(2, T_FFN0, 0)
            for t in range(TILES):
                for i in range(2):
                    pe.wait_ge(lo_ready, FFN0 + i + 1)
                    pe.wait_ge(xlo_ready, TR0[T_FFN0] + 2 * t + i + 1)
                    last = in_tile(FFN0 + i, 0, t, B_U, i)
                    if t == 1:
                        last.then_inc(units_done, 1)
                    elif i == 0:
                        norm_transposed(2, T_FFN0, 1)
            unit_in(FFN0 + 2, 0, TILES, B_G, 0)
            unit_in(FFN0 + 3, 0, TILES, B_G, 1, g_done)
            pe.wait_ge(zero_set, 1)
            clear_y(TILES)
            for t in range(TILES):
                hidden_t(t, t)
            with pe.Fori(1, STEPS) as s:
                products_in(FFN0 - 2, s, TILES, s * TILES)
                unit_out(FFN0 + 2, s, TILES, 0)
                for t in range(TILES):
                    hidden_t(t, s * TILES + t)
                unit_out(FFN0 + 3, s, TILES, 1)
            pe.wait_ge(tlo_ready, EV_MOE)
            for t in range(TILES):
                for i in range(2):
                    u = FFN0 + FFN_UNITS - 2 + i
                    pe.wait_ge(lo_ready, u + 1)
                    last = out_tile(u, t, i, True)
                    if t == 1:
                        last.then_inc(units_done, 1)
                    elif i == 1:
                        last.then_inc(y0_done, 1)
            norm_transposed(3, T_MIX1, 0)
            chunk(C_DI, T_MIX1, lambda: norm_transposed(3, T_MIX1, 1))
            for c in range(C_DI + 1, C_DO):
                chunk(c)
            pe.wait_ge(ev_act, ACT_EV[C_DO - 1])
            pe.wait_ge(ev_dve, DVE_EV[C_DO - 1])
            attention(1)
            mixed_transposed(1, T_CAT1, 0)
            pe.wait_ge(ev_act, ACT_EV[C_DO - 1])
            pe.wait_ge(ev_dve, DVE_EV[C_DO - 1])
            for t in range(TILES):
                for c in (C_DO, C_DO + 1):
                    u = FIRST[c]
                    pe.wait_ge(lo_ready, u + 1)
                    pe.wait_ge(xlo_ready, TR0[T_CAT1] + t + 1)
                    for kt in range(4):
                        cols = slice(kt * 512, (kt + 1) * 512)
                        last = three(ps[:, 4 + 2 * (c % 2) + t, :], xhi[:, kt, t * P:(t + 1) * P],
                                     xlo[:, kt, t * P:(t + 1) * P], whi[:, u % CUT, cols], wlo[:, u % CUT, cols],
                                     kt == 0, kt == 3)
                    last.then_inc(chunk_done if t == 0 else units_done, 1)
                    if t == 0 and c == C_DO:
                        mixed_transposed(1, T_CAT1, 1)
            pe.wait_ge(rw_in, 16)
            for t in range(TILES):
                norm_transposed(4, T_ROUTE, t)
                for kt in range(KT):
                    if kt % 4 == 0:
                        pe.wait_ge(xtf_ready, 2 * t + kt // 4 + 1)
                    last = pe.matmul(ps[:, B_LG[t], 0:NE], xtf[:, kt, t * P:(t + 1) * P], rw[:, kt, :],
                                     start=kt == 0, stop=kt == KT - 1)
            last.then_inc(logit_done, 1)
            pe.wait_ge(rank_in, 1)
            sel = [rt[:, 336 + NE * t:336 + NE * (t + 1)] for t in range(TILES)]
            pe.matmul(ps[:, B_RANK, 2 * NE:3 * NE], ones, sel[0], start=True, stop=False)
            pe.matmul(ps[:, B_RANK, 2 * NE:3 * NE], ones, sel[1], start=False, stop=True)
            pe.matmul(ps[:, B_RANK, 0:NE], before, sel[0], start=True, stop=True)
            pe.matmul(ps[:, B_RANK, NE:2 * NE], ones, sel[0], start=True, stop=False)
            pe.matmul(ps[:, B_RANK, NE:2 * NE], before, sel[1], start=False, stop=True).then_inc(rank_done, 1)

            def gather(q):
                pe.wait_ge(pick_ready, 2 * q + 2)
                for kt in range(KT):
                    dst = ps[:, B_X[kt // 4], kt % 4 * P:(kt % 4 + 1) * P]
                    for n, (t, part) in enumerate([(t, part) for t in range(TILES) for part in (nhi, nlo)]):
                        last = pe.matmul(dst, part[:, t, kt * P:(kt + 1) * P], pick[:, t, :], start=n == 0, stop=n == 3)
                    if kt % 4 == 3:
                        last.then_inc(gx_done, 1)

            def gather_put(q):
                for t in range(TILES):
                    pe.transpose(ps[:, B_PUT, t * P:(t + 1) * P], pick[:, t, :].bitcast(F32), ident)
                pe.wait_ge(comb_ready, 1)
                for t in range(TILES):
                    last = pe.matmul(ps[:, B_PUT, SEQ:SEQ + 1], pick[:, t, :].bitcast(F32), comb[:, t, bass.ds(q, 1)],
                                     start=t == 0, stop=t == 1)
                last.then_inc(put_done, 1)

            def scatter(prev, final=False):
                pe.wait_ge(put_now, 2 * prev + 2)
                pe.wait_ge(ylo_ready, 2 * prev + 2)
                if not final:
                    pe.wait_ge(put_out, 2 * prev + 4)
                for n in range(4):
                    t, b = n // 2, n % 2
                    pe.matmul(ps[:, B_SC[n], :], put[:, t * P:(t + 1) * P], yhi[:, b * 512:(b + 1) * 512],
                              start=True, stop=False)
                    pe.matmul(ps[:, B_SC[n], :], put[:, t * P:(t + 1) * P], ylo[:, b * 512:(b + 1) * 512],
                              start=False, stop=True).then_inc(sc_done, 1)

            def expert(prev=None, final=False):
                first = prev is None
                job = 0 if first else prev + 1
                r = job * STEPS
                if first:
                    for i in range(2):
                        pe.wait_ge(gxlo, i + 1)
                        unit_in(MOE0 + i, 0, 1, B_U, i)
                    for i in range(2):
                        unit_in(MOE0 + 2 + i, 0, 1, B_G, i)
                    gather_put(0)
                else:
                    pe.wait_ge(gxlo, 2 * job + 2)
                    products_in(MOE0, r, 1)
                    scatter(prev)
                clear_y(1)
                hidden_t(0, r + EV_MOE)
                with pe.Fori(1, STEPS) as s:
                    rs = s + job * STEPS
                    products_in(MOE0 - 2, rs, 1, rs + EV_MOE)
                    unit_out(MOE0 + 2, rs, 1, 0)
                    hidden_t(0, rs + EV_MOE)
                    unit_out(MOE0 + 3, rs, 1, 1)
                if not first:
                    pe.wait_ge(h_added, 4 * prev + 4)
                if not final:
                    gather(job + 1)
                    gather_put(job + 1)
                pe.wait_ge(tlo_ready, r + EV_MOE + STEPS)
                for i in range(2):
                    unit_out(MOE0 + FFN_UNITS - 2 + i, r, 1, i, True)

            pe.wait_ge(nlo_ready, 2)
            pe.wait_ge(zero_set, 2)
            gather(0)
            expert()
            pe.wait_ge(table_ready, 1)
            middle = pe.value_load(jobs_i[0:1, 0:1], min_val=NE - 2, max_val=JOBS - 2)
            with pe.Fori(0, middle) as prev:
                expert(prev)
            expert(middle, True)
            scatter(middle + 1, True)


_INS = ["x", "mem", "rel_bias_table", "mem_norm", "norm_mix", "norm_ffn", "final_norm", "swa_w_in", "swa_sinks",
        "swa_w_mem_kv", "swa_w_out", "dil_w_in", "dil_w_mem_kv", "dil_w_out", "ffn_gate", "ffn_up", "ffn_down",
        "router", "moe_gate", "moe_up", "moe_down"]


def kernel(**inputs):
    import concourse.bacc as bacc
    from concourse.bass_utils import run_bass_kernel_spmd

    nc = bacc.Bacc("TRN2", target_bir_lowering=False, num_devices=1)
    index_mats, bias_onehot = shape_constants()
    arrays = {name: np.ascontiguousarray(inputs[name]) for name in _INS}
    arrays["index_mats"], arrays["bias_onehot"] = index_mats, bias_onehot
    args = [nc.dram_tensor(f"in_{name}", a.shape, mybir.dt.from_np(a.dtype), kind="ExternalInput").ap()
            for name, a in arrays.items()]
    out = nc.dram_tensor("out_trunk", (1, SEQ, D), F32, kind="ExternalOutput").ap()
    trunk(nc, *args, out)
    result = run_bass_kernel_spmd(nc, [{f"in_{name}": a for name, a in arrays.items()}], core_ids=[0])
    return result.results[0]["out_trunk"]
```
